# Optimizing a Trainium2 kernel written in Bass

```python
import jax, jax.numpy as jnp
from jax import lax
import numpy as np

D_MODEL = 1024
BATCH = 1
SEQ = 512
DEPTH = 2

N_A_LAYERS = DEPTH // 2
N_B_LAYERS = DEPTH - N_A_LAYERS
CONV_WIDTH = 3
N_HEADS = 16
HEAD_DIM = D_MODEL // N_HEADS
N_KV_HEADS = 4
GQA_GROUP = N_HEADS // N_KV_HEADS
CMP_BLOCK = 32
CMP_STRIDE = 16
CMP_HIDDEN = 4 * HEAD_DIM
SEL_BLOCK = 64
SEL_TOP = 16
WINDOW = 512
Q_BLOCK = 128
N_EXPERTS = 16
N_GROUPS = 4
EXPERTS_PER_GROUP = N_EXPERTS // N_GROUPS
TOP_K = 2
D_FF_EXPERT = D_MODEL // 2
ALPHA = (2 * DEPTH) ** 0.25
BETA = (8 * DEPTH) ** -0.25
LN_EPS = 1e-5
NEG = -1e30
FORCE = 1e9

kernel_name = "hybrid_shortconv_nsa_yoco_moe"

def layer_norm(x, g, b):
    xf = x.astype(jnp.float32)
    mu = jnp.mean(xf, -1, keepdims=True)
    var = jnp.mean(jnp.square(xf - mu), -1, keepdims=True)
    y = (xf - mu) * lax.rsqrt(var + LN_EPS)
    return (y * g.astype(jnp.float32) + b.astype(jnp.float32)).astype(x.dtype)

def masked_softmax(s, mask, axis):
    s = jnp.where(mask, s, NEG)
    m = jnp.max(s, axis=axis, keepdims=True)
    e = jnp.where(mask, jnp.exp(s - m), 0.0)
    return e / jnp.maximum(jnp.sum(e, axis=axis, keepdims=True), 1e-30)

def short_conv_mixer(u, w_in, conv_w, conv_b, w_out):
    bch = u @ w_in
    b_gate, c_gate, h = jnp.split(bch, 3, axis=-1)
    z = c_gate * h
    z = lax.conv_general_dilated(
        z, conv_w[:, None, :], window_strides=(1,),
        padding=[(CONV_WIDTH - 1, 0)],
        dimension_numbers=("NWC", "WIO", "NWC"),
        feature_group_count=D_MODEL) + conv_b
    return (b_gate * z) @ w_out

def nsa_shared_kv(s, w_kv, cmp_pe, cmp_w1, cmp_b1, cmp_w2, cmp_b2):
    B, S, _ = s.shape
    kv = (s @ w_kv).reshape(B, S, 6, N_KV_HEADS, HEAD_DIM)
    kv = jnp.transpose(kv, (2, 0, 3, 1, 4))
    k_c, v_c, k_s, v_s, k_w, v_w = kv[0], kv[1], kv[2], kv[3], kv[4], kv[5]
    n_cmp = (S - CMP_BLOCK) // CMP_STRIDE + 1
    idx = jnp.arange(n_cmp)[:, None] * CMP_STRIDE + jnp.arange(CMP_BLOCK)[None, :]

    def compress(t, i):
        blocks = t[:, :, idx] + cmp_pe[i]
        flat = blocks.reshape(B, N_KV_HEADS, n_cmp, CMP_BLOCK * HEAD_DIM)
        hdn = jax.nn.gelu(flat @ cmp_w1[i] + cmp_b1[i])
        return hdn @ cmp_w2[i] + cmp_b2[i]

    kc = compress(k_c, 0)
    vc = compress(v_c, 1)
    n_sel = S // SEL_BLOCK
    ks = k_s.reshape(B, N_KV_HEADS, n_sel, SEL_BLOCK, HEAD_DIM)
    vs = v_s.reshape(B, N_KV_HEADS, n_sel, SEL_BLOCK, HEAD_DIM)
    pad = ((0, 0), (0, 0), (WINDOW, 0), (0, 0))
    kw = jnp.pad(k_w, pad)
    vw = jnp.pad(v_w, pad)
    return kc, vc, ks, vs, kw, vw

def nsa_mixer(u, w_qg, b_g, w_o, kc, vc, ks, vs, kw, vw):
    B, S, _ = u.shape
    f32 = jnp.float32
    qg = u @ w_qg
    q = qg[..., :N_HEADS * HEAD_DIM].reshape(B, S, N_KV_HEADS, GQA_GROUP, HEAD_DIM)
    q = jnp.transpose(q, (0, 2, 3, 1, 4)) * (HEAD_DIM ** -0.5)
    g = jax.nn.sigmoid((qg[..., N_HEADS * HEAD_DIM:] + b_g).astype(f32))
    g = jnp.transpose(g.reshape(B, S, N_KV_HEADS, GQA_GROUP, 3), (0, 2, 3, 1, 4))

    n_cmp = kc.shape[2]
    n_sel = ks.shape[2]
    cmp_start = jnp.arange(n_cmp) * CMP_STRIDE
    cmp_end = cmp_start + CMP_BLOCK - 1
    sel_start = jnp.arange(n_sel) * SEL_BLOCK
    overlap = jnp.clip(
        jnp.minimum(cmp_start[:, None] + CMP_BLOCK, sel_start[None, :] + SEL_BLOCK)
        - jnp.maximum(cmp_start[:, None], sel_start[None, :]), 0, None).astype(f32) / CMP_BLOCK
    n_top = min(SEL_TOP, n_sel)
    bi = jnp.arange(B)[:, None, None, None]
    hi = jnp.arange(N_KV_HEADS)[None, :, None, None]
    jsel = jnp.arange(n_sel)

    def block(i):
        s0 = i * Q_BLOCK
        qb = lax.dynamic_slice_in_dim(q, s0, Q_BLOCK, axis=3)
        gb = lax.dynamic_slice_in_dim(g, s0, Q_BLOCK, axis=3)
        t = s0 + jnp.arange(Q_BLOCK)
        sc = jnp.einsum("bhgqd,bhnd->bhgqn", qb, kc).astype(f32)
        pc = masked_softmax(sc, cmp_end[None, :] <= t[:, None], -1)
        o_c = jnp.einsum("bhgqn,bhnd->bhgqd", pc.astype(vc.dtype), vc)
        imp = jnp.einsum("bhgqn,nj->bhqj", pc, overlap)
        cur = t // SEL_BLOCK
        allowed = jsel[None, :] <= cur[:, None]
        forced = (jsel[None, :] == 0) | (jsel[None, :] == cur[:, None]) | (jsel[None, :] == cur[:, None] - 1)
        score = jnp.where(forced & allowed, FORCE, jnp.where(allowed, imp, NEG))
        top_val, top_idx = lax.top_k(score, n_top)
        sel_ok = top_val > 0.5 * NEG
        kg = ks[bi, hi, top_idx]
        vg = vs[bi, hi, top_idx]
        kpos = top_idx[..., None] * SEL_BLOCK + jnp.arange(SEL_BLOCK)
        ms = sel_ok[..., None] & (kpos <= t[None, None, :, None, None])
        ssel = jnp.einsum("bhgqd,bhqnkd->bhgqnk", qb, kg).astype(f32)
        ps = masked_softmax(ssel, ms[:, :, None], (-2, -1))
        o_s = jnp.einsum("bhgqnk,bhqnkd->bhgqd", ps.astype(vg.dtype), vg)
        kwb = lax.dynamic_slice_in_dim(kw, s0, WINDOW + Q_BLOCK, axis=2)
        vwb = lax.dynamic_slice_in_dim(vw, s0, WINDOW + Q_BLOCK, axis=2)
        wpos = s0 - WINDOW + jnp.arange(WINDOW + Q_BLOCK)
        mw = (wpos[None, :] <= t[:, None]) & (wpos[None, :] > t[:, None] - WINDOW) & (wpos[None, :] >= 0)
        sw = jnp.einsum("bhgqd,bhkd->bhgqk", qb, kwb).astype(f32)
        pw = masked_softmax(sw, mw, -1)
        o_w = jnp.einsum("bhgqk,bhkd->bhgqd", pw.astype(vwb.dtype), vwb)
        o = gb[..., 0:1] * o_c + gb[..., 1:2] * o_s + gb[..., 2:3] * o_w
        return o.astype(u.dtype)

    o = lax.map(block, jnp.arange(S // Q_BLOCK))
    o = jnp.transpose(o, (1, 0, 4, 2, 3, 5)).reshape(B, S, N_HEADS * HEAD_DIM)
    return o @ w_o

def grouped_moe(u, router_w, router_bias, w_gu, w_down):
    B, S, D = u.shape
    f32 = jnp.float32
    tok = u.reshape(-1, D)
    aff = jax.nn.softmax((tok @ router_w).astype(f32), axis=-1)
    biased = aff + router_bias.astype(f32)
    grp_score = lax.top_k(biased.reshape(-1, N_GROUPS, EXPERTS_PER_GROUP), TOP_K)[0].sum(-1)
    best = jnp.argmax(grp_score, axis=-1)
    in_grp = (jnp.arange(N_EXPERTS) // EXPERTS_PER_GROUP)[None, :] == best[:, None]
    _, idx = lax.top_k(jnp.where(in_grp, biased, NEG), TOP_K)
    w = jnp.take_along_axis(aff, idx, axis=-1)
    w = w / jnp.sum(w, -1, keepdims=True)
    comb = jnp.sum(jax.nn.one_hot(idx, N_EXPERTS, dtype=f32) * w[..., None], axis=-2)
    out = jnp.zeros_like(tok)
    for e in range(N_EXPERTS):
        gate, up = jnp.split(tok @ w_gu[e], 2, axis=-1)
        out = out + comb[:, e:e + 1].astype(tok.dtype) * ((jax.nn.silu(gate) * up) @ w_down[e])
    return out.reshape(B, S, D)

def setup_inputs(seed: int = 0) -> dict:
    key = jax.random.key(seed)
    ks = jax.random.split(key, 24)
    f32 = jnp.float32
    D = D_MODEL
    nrm = lambda k, shape, s: jax.random.normal(k, shape, f32) * s
    gate_pattern = jnp.repeat(jnp.array([0.0, 0.0, 1.0, 0.0, 0.0, 1.0], f32), D)
    return {
        "x": nrm(ks[0], (BATCH, SEQ, D), 1.0),
        "c": nrm(ks[1], (BATCH, D), 1.0),
        "ada_w": nrm(ks[2], (DEPTH, D, 6 * D), 0.1 * D ** -0.5),
        "ada_b": gate_pattern[None, :] + nrm(ks[3], (DEPTH, 6 * D), 0.02),
        "ln_g": 1.0 + nrm(ks[4], (DEPTH, 2, D), 0.02),
        "ln_b": nrm(ks[5], (DEPTH, 2, D), 0.02),
        "conv_w_in": nrm(ks[6], (N_A_LAYERS, D, 3 * D), D ** -0.5),
        "conv_w": nrm(ks[7], (N_A_LAYERS, CONV_WIDTH, D), CONV_WIDTH ** -0.5),
        "conv_b": nrm(ks[8], (N_A_LAYERS, D), 0.02),
        "conv_w_out": nrm(ks[9], (N_A_LAYERS, D, D), BETA * D ** -0.5),
        "w_kv": nrm(ks[10], (D, 6 * N_KV_HEADS * HEAD_DIM), D ** -0.5),
        "cmp_pe": nrm(ks[11], (2, CMP_BLOCK, HEAD_DIM), 0.02),
        "cmp_w1": nrm(ks[12], (2, CMP_BLOCK * HEAD_DIM, CMP_HIDDEN), (CMP_BLOCK * HEAD_DIM) ** -0.5),
        "cmp_b1": nrm(ks[13], (2, CMP_HIDDEN), 0.02),
        "cmp_w2": nrm(ks[14], (2, CMP_HIDDEN, HEAD_DIM), CMP_HIDDEN ** -0.5),
        "cmp_b2": nrm(ks[15], (2, HEAD_DIM), 0.02),
        "w_qg": nrm(ks[16], (N_B_LAYERS, D, N_HEADS * HEAD_DIM + 3 * N_HEADS), D ** -0.5),
        "b_g": nrm(ks[17], (N_B_LAYERS, 3 * N_HEADS), 0.02),
        "w_o": nrm(ks[18], (N_B_LAYERS, N_HEADS * HEAD_DIM, D), BETA * (N_HEADS * HEAD_DIM) ** -0.5),
        "router_w": nrm(ks[19], (D, N_EXPERTS), D ** -0.5),
        "router_bias": nrm(ks[20], (N_EXPERTS,), 0.01),
        "w_gu": nrm(ks[21], (DEPTH, N_EXPERTS, D, 2 * D_FF_EXPERT), D ** -0.5),
        "w_down": nrm(ks[22], (DEPTH, N_EXPERTS, D_FF_EXPERT, D), BETA * D_FF_EXPERT ** -0.5),
    }

def reference(x, c, ada_w, ada_b, ln_g, ln_b, conv_w_in, conv_w, conv_b, conv_w_out,
              w_kv, cmp_pe, cmp_w1, cmp_b1, cmp_w2, cmp_b2, w_qg, b_g, w_o,
              router_w, router_bias, w_gu, w_down):
    mod = jnp.einsum("bd,lde->lbe", jax.nn.silu(c), ada_w) + ada_b[:, None, :]
    shared = None
    for l in range(DEPTH):
        sh1, sc1, g1, sh2, sc2, g2 = jnp.split(mod[l][:, None, :], 6, axis=-1)
        u = x * (1.0 + sc1) + sh1
        if l < N_A_LAYERS:
            y = short_conv_mixer(u, conv_w_in[l], conv_w[l], conv_b[l], conv_w_out[l])
        else:
            if l == N_A_LAYERS:
                shared = nsa_shared_kv(x, w_kv, cmp_pe, cmp_w1, cmp_b1, cmp_w2, cmp_b2)
            lb = l - N_A_LAYERS
            y = nsa_mixer(u, w_qg[lb], b_g[lb], w_o[lb], *shared)
        x = layer_norm(ALPHA * x + g1 * y, ln_g[l, 0], ln_b[l, 0])
        u = x * (1.0 + sc2) + sh2
        y = grouped_moe(u, router_w, router_bias, w_gu[l], w_down[l])
        x = layer_norm(ALPHA * x + g2 * y, ln_g[l, 1], ln_b[l, 1])
    return x


_drawn_inputs = setup_inputs


def setup_inputs(seed=0):
    import zlib

    import numpy as np

    out = dict(_drawn_inputs(seed))
    spreads = {}
    factors = {'cmp_pe': 13.681, 'cmp_b1': 5.288, 'cmp_b2': 4.704, 'b_g': 26.675}
    for name, (base, spread) in spreads.items():
        noise = np.random.default_rng([zlib.crc32(name.encode()), seed]).standard_normal(out[name].shape)
        drawn = base * np.exp(spread * noise) if base else spread * noise
        out[name] = __import__('jax').numpy.asarray(drawn.astype(out[name].dtype))
    for name, factor in factors.items():
        out[name] = (out[name] * factor).astype(out[name].dtype)
    return out
```

```python
from contextlib import ExitStack

import concourse.bass as bass
from concourse import mybir

F32 = mybir.dt.float32
F32R = mybir.dt.float32r
BF16 = mybir.dt.bfloat16
U32 = mybir.dt.uint32
ALU = mybir.AluOpType
ACT = mybir.ActivationFunctionType
AX_X = mybir.AxisListType.X

P = 128
BANK = 512
D = 1024
SEQ = 512
DEPTH = 2
KD = D // P
TT = SEQ // P
NH, HD, NKV = 16, 64, 4
GQA = NH // NKV
NCMP, CMP_STRIDE, CMP_BLOCK = 31, 16, 32
NE, NG, EPG, FF = 16, 4, 4, 512
ALPHA = (2 * DEPTH) ** 0.25
LN_EPS = 1e-5
NEG = -1e30
BLK = 2048
NRAW = 6
NSPLIT = 3
NADA = 4
CAP = 128
LIMIT = CAP
EBLK = 6
SH1, SC1, G1, SH2, SC2, G2 = range(6)
C_CW, C_CB, C_B1, C_B2, C_C, C_PE, C_PES = 0, 24, 32, 36, 37, 45, 77


def hybrid_trunk(nc, x, c, ada_w, ada_b, ln_g, ln_b, conv_w_in, conv_w, conv_b, conv_w_out,
                 w_kv, cmp_pe, cmp_w1, cmp_b1, cmp_w2, cmp_b2, w_qg, b_g, w_o,
                 router_w, router_bias, w_gu, w_down, out, scratch):
    def cols4(w, kh, c0):
        return w.rearrange("(k p) n -> p k n", p=P)[:, 4 * kh:4 * kh + 4, c0:c0 + BANK]

    conv_in = [cols4(conv_w_in[0], kh, part * D + half * BANK)
               for half in range(2) for part in (1, 2, 0) for kh in range(2)]
    conv_out = [cols4(conv_w_out[0], kh, n * BANK) for n in range(2) for kh in range(2)]
    kv = [cols4(w_kv, kh, g * BANK) for g in range(3) for kh in range(2)]
    cmp1 = [cmp_w1[i].rearrange("(k p) n -> p k n", p=P)[:, 8 * kh:8 * kh + 8, :]
            for i in range(2) for kh in range(2)]
    qw = [cols4(w_qg[0], kh, n * BANK) for n in range(2) for kh in range(2)]
    ow = [cols4(w_o[0], kh, n * BANK) for n in range(2) for kh in range(2)]
    B_CONV = 0
    B_COUT = B_CONV + len(conv_in)
    B_MOE = [B_COUT + len(conv_out), 0]
    B_KV = B_MOE[0] + NE * EBLK
    B_CMP = B_KV + len(kv)
    B_Q = B_CMP + len(cmp1)
    B_O = B_Q + len(qw)
    B_MOE[1] = B_O + len(ow)
    B_END = B_MOE[1] + NE * EBLK

    def shape_block(ap, src):
        return ap.rearrange("p (k n) -> p k n", n=src.shape[2])

    with ExitStack() as ctx:
        place = [(nc.sbuf_base + 31) // 32 * 32]

        def region(nbytes):
            at = place[0]
            place[0] += (nbytes + 31) // 32 * 32
            return at

        def at(name, shape, dt, offset):
            return nc.alloc_sbuf_tensor_at(name, shape, dt, offset=offset)

        def new(name, shape, dt):
            n = 1
            for s in shape[1:]:
                n *= s
            return at(name, shape, dt, region(n * (2 if dt == BF16 else 4)))

        def sem(name):
            return ctx.enter_context(nc.semaphore(name))

        class Count:
            pool = {}

            def __init__(self, name, total=0):
                if name not in Count.pool:
                    Count.pool[name] = [sem(name), 0]
                self.sem, self.base = Count.pool[name]
                Count.pool[name][1] += total

            def at(self, value):
                return self.sem, self.base + value

        w_lo_at = place[0]
        raw = new("raw", [P, NRAW, BLK], F32)
        w_lo = at("w_lo", [P, NRAW, BLK], F32R, w_lo_at)
        w_hi = new("w_hi", [P, NSPLIT, BLK], F32R)
        KB = 1024
        X0 = region(16416)
        U0 = region(32 * KB)
        V0 = region(32 * KB)
        S0 = region(40 * KB + 128)
        A0 = region(12 * KB)
        rows = at("rows", [P, 3, D], F32, A0)
        ident = new("ident", [P, P], F32)
        identb = new("identb", [P, P], BF16)
        ones_col = new("ones_col", [P, 1], F32)
        eps_col = new("eps_col", [P, 1], F32)
        ones_b = new("ones_b", [P, P], BF16)
        before_b = new("before_b", [P, P], BF16)
        small = new("small", [P, P], F32)
        silu_c = new("silu_c", [P, KD], F32)
        ln_stat = new("ln_stat", [P, TT, 12], F32)
        ln_mv = new("ln_mv", [P, TT, 8], F32)

        xt = at("xt", [P, TT, D], F32, X0)
        z = at("z", [P, 4, SEQ + 2], F32, X0)
        ct = at("ct", [P, 4, SEQ], F32, X0 + 4 * (SEQ + 2) * 4)
        u_hi = at("u_hi", [P, KD, SEQ], F32R, U0)
        u_lo = at("u_lo", [P, KD, SEQ], F32R, U0 + 16 * KB)
        v_hi = at("v_hi", [P, KD, SEQ], F32R, V0)
        v_lo = at("v_lo", [P, KD, SEQ], F32R, V0 + 16 * KB)
        ada = at("ada", [P, NADA, D], F32, S0)
        acc = at("acc", [P, 2, D], F32, S0 + 16 * KB)
        bias0 = at("bias0", [P, D], F32, S0 + 24 * KB)
        modrow = at("modrow", [P, D], F32, S0 + 28 * KB)
        ada2 = at("ada2", [P, NADA, D], F32, w_lo_at + 4 * BLK * 4)
        acc2 = at("acc2", [P, 4, D], F32, X0)
        us = at("us", [P, 2, D], F32, S0 + 32 * KB)
        small_rows = at("small_rows", [P, P], F32, U0)

        bank = [ctx.enter_context(nc.psum_tensor(f"bank{i}", [P, BANK], F32)) for i in range(8)]

        raw_in = [sem(f"raw_in{i}") for i in range(NRAW)]
        hi_done, lo_done, blk_used = sem("hi_done"), sem("lo_done"), sem("blk_used")
        x_in = sem("x_in")
        small_clear, small_in, small_t, small_ready = (sem("small_clear"), sem("small_in"),
                                                       sem("small_t"), sem("small_ready"))
        silu_ready = sem("silu_ready")
        const_step, const_v = sem("const_step"), sem("const_v")
        row_in = [sem(f"row_in{i}") for i in range(3)]
        row_used = sem("row_used")
        conv_mm = sem("conv_mm")
        dve_step, act_step = sem("dve_step"), sem("act_step")
        x_back = sem("x_back")
        stored = sem("stored")

        row_plan = []
        for l in range(DEPTH):
            row_plan += [("mod", l, SC1), ("mod", l, SH1), ("mod", l, G1), ("g", l, 0), ("b", l, 0),
                         ("mod", l, SC2), ("mod", l, SH2), ("mod", l, G2), ("g", l, 1), ("b", l, 1)]
        mod_order = [(l, v) for l in range(DEPTH) for v in (SC1, SH1, G1, SC2, SH2, G2)]
        R = {k: i for i, k in enumerate(row_plan)}

        def row(key):
            return rows[:, R[key] % 3, :]

        def wait_row(eng, key):
            eng.wait_ge(row_in[R[key] % 3], 16 * (R[key] // 3 + 1))

        def load_block(sp, b, src):
            if b >= NRAW:
                sp.wait_ge(blk_used, b - NRAW + 1)
            sp.dma_start(shape_block(raw[:, b % NRAW, :], src), src).then_inc(raw_in[b % NRAW], 16)

        def split_hi(act, b):
            act.wait_ge(raw_in[b % NRAW], 16 * (b // NRAW + 1))
            if b >= NSPLIT:
                act.wait_ge(blk_used, b - NSPLIT + 1)
            nc.scalar.activation(w_hi[:, b % NSPLIT, :], raw[:, b % NRAW, :], ACT.Copy).then_inc(hi_done, 1)

        def split_lo(dve, b):
            dve.wait_ge(hi_done, b + 1)
            s = b % NRAW
            nc.vector.tensor_tensor(w_lo[:, s, :], raw[:, s, :], w_hi[:, b % NSPLIT, :].bitcast(F32),
                                    ALU.subtract).then_inc(lo_done, 1)

        def mm3(o, lh, ll, rh, rl, start, stop):
            nc.tensor.matmul(o, lh, rl, start=start, stop=False)
            nc.tensor.matmul(o, ll, rh, start=False, stop=False)
            return nc.tensor.matmul(o, lh, rh, start=False, stop=stop)

        def link(eng, count, step, ins):
            ins.then_inc(step, 1)
            count[0] += 1
            eng.wait_ge(step, count[0])

        dve_n, act_n = [0], [0]

        def small_loads(eng):
            eng.wait_ge(small_clear, 1)
            half_swap = cmp_pe.rearrange("i (a h) d -> (i a) h d", h=2)
            for dst, src in (
                    (small_rows[C_CW:C_CW + 24, :], conv_w[0].rearrange("w (k p) -> (w k) p", p=P)),
                    (small_rows[C_CB:C_CB + 8, :], conv_b[0].rearrange("(k p) -> k p", p=P)),
                    (small_rows[C_B1:C_B1 + 4, :], cmp_b1.rearrange("i (h p) -> (i h) p", p=P)),
                    (small_rows[C_B2:C_B2 + 1, 0:HD], cmp_b2[0:1, :]),
                    (small_rows[C_C:C_C + KD, :], c[0].rearrange("(k p) -> k p", p=P)),
                    (small_rows[C_PE:C_PE + 32, :], cmp_pe.rearrange("i (a h) d -> (i a) (h d)", h=2)),
                    (small_rows[C_PES:C_PES + 32, 0:HD], half_swap[:, 1, :]),
                    (small_rows[C_PES:C_PES + 32, HD:P], half_swap[:, 0, :])):
                eng.dma_start(dst, src).then_inc(small_in, 16)

        N_SMALL = 8

        def constants(pool):
            nc.gpsimd.memset(ident[:], 0.0).then_inc(const_step, 1)
            nc.gpsimd.memset(ones_b[:], 1.0).then_inc(const_step, 1)
            pool.wait_ge(const_step, 2)
            nc.gpsimd.affine_select(out=ident[:], in_=ident[:], compare_op=ALU.not_equal, fill=1.0, base=0,
                                    pattern=[[-1, P]], channel_multiplier=1).then_inc(const_step, 1)
            nc.gpsimd.affine_select(out=before_b[:], in_=ones_b[:], compare_op=ALU.is_gt, fill=0.0, base=0,
                                    pattern=[[1, P]], channel_multiplier=-1).then_inc(const_step, 1)
            pool.wait_ge(const_step, 4)
            nc.gpsimd.tensor_copy(identb[:], ident[:]).then_inc(const_step, 1)

        N_CONST = 5

        class AdaPass:
            def __init__(self, j0, j1, ring, accs, bias, row_, n_ring, n_acc):
                self.j0, self.j1, self.ring, self.accs, self.bias, self.row = j0, j1, ring, accs, bias, row_
                self.n_ring, self.n_acc = n_ring, n_acc
                n = j1 - j0
                self.loaded = [Count(f"ada_in{i}", 16 * n * KD // n_ring) for i in range(n_ring)]
                self.cleared = Count("ada_cleared", n if bias is None else 1)
                self.bias_in, self.mac = Count("ada_bias_in", 16 * n), Count("ada_mac", n * KD)
                self.summed, self.row_made, self.stored = (Count("mod_sum", n), Count("mod_row", 2 * n),
                                                           Count("mod_stored", 16 * n))

        ada_a = AdaPass(0, 8, ada, acc, bias0, modrow, NADA, 2)
        ada_b2 = AdaPass(8, 12, ada2, acc2, None, acc2, NADA, 4)

        def ada_loads(pool, s, j):
            l, v = mod_order[j]
            n = j - s.j0
            if s.bias is None:
                pool.wait_ge(*s.cleared.at(n + 1))
            elif n >= 1:
                pool.wait_ge(*s.mac.at(KD * (n - 1) + 1))
            else:
                pool.wait_ge(*s.cleared.at(1))
            pool.dma_start((s.accs[0:1, n % s.n_acc, :] if s.bias is None else s.bias[0:1, :]), ada_b[l:l + 1, v * D:(v + 1) * D]).then_inc(s.bias_in.sem, 16)
            for k in range(KD):
                t = n * KD + k
                if t >= s.n_ring:
                    pool.wait_ge(*s.mac.at(t - s.n_ring + 1))
                pool.dma_start(s.ring[:, t % s.n_ring, :], ada_w[l, k * P:(k + 1) * P, v * D:(v + 1) * D]
                               ).then_inc(s.loaded[t % s.n_ring].sem, 16)

        def mod_store(pool, s, j):
            pool.wait_ge(*s.row_made.at(2 * (j - s.j0 + 1)))
            row_ap = s.row[0:1, (j - s.j0) % s.n_acc, :] if s.bias is None else s.row[0:1, :]
            pool.dma_start(scratch["mods"][j:j + 1, :], row_ap).then_inc(s.stored.sem, 16)

        def row_load(pool, r):
            kind, l, v = row_plan[r]
            if kind == "mod":
                j = mod_order.index((l, v))
                s = ada_a if j < ada_a.j1 else ada_b2
                pool.wait_ge(*s.stored.at(16 * (j - s.j0 + 1)))
                src = scratch["mods"][j, :]
            else:
                src = (ln_g if kind == "g" else ln_b)[l, v]
            if r >= 3:
                pool.wait_ge(row_used, r - 2)
            pool.dma_start(rows[:, r % 3, :], src.partition_broadcast(P)).then_inc(row_in[r % 3], 16)

        def ada_clear(dve, s, n):
            if n >= s.n_acc:
                dve.wait_ge(*s.stored.at(16 * (n - s.n_acc + 1)))
            nc.vector.memset(s.accs[:, n % s.n_acc, :], 0.0).then_inc(s.cleared.sem, 1)

        def ada_macs(dve, s, t0, n):
            for t in range(t0, min(t0 + n, (s.j1 - s.j0) * KD)):
                j, k = t // KD, t % KD
                dve.wait_ge(*s.loaded[t % s.n_ring].at(16 * (t // s.n_ring + 1)))
                if k == 0 and s.bias is None and j + 1 < s.j1 - s.j0:
                    ada_clear(dve, s, j + 1)
                if k == 0:
                    dve.wait_ge(*s.bias_in.at(16 * (j + 1)))
                    if s.bias is not None and j >= s.n_acc:
                        dve.wait_ge(*s.summed.at(j - s.n_acc + 1))
                if t:
                    dve.wait_ge(*s.mac.at(t))
                a = s.accs[:, j % s.n_acc, :]
                nc.vector.scalar_tensor_tensor(out=a, in0=s.ring[:, t % s.n_ring, :], scalar=silu_c[:, k:k + 1],
                                               in1=a if k or s.bias is None else s.bias[:], op0=ALU.mult,
                                               op1=ALU.add).then_inc(s.mac.sem, 1)

        def mod_sums(pe, s, j, banks):
            n = j - s.j0
            pe.wait_ge(*s.mac.at((n + 1) * KD))
            if n >= 1:
                pe.wait_ge(*s.row_made.at(2 * n))
            for h in range(2):
                m = nc.tensor.matmul(banks[h][0:1, :], ones_col[:, 0:1],
                                     s.accs[:, n % s.n_acc, h * BANK:(h + 1) * BANK], start=True, stop=True)
            m.then_inc(s.summed.sem, 1)

        def mod_rows(act, s, j, banks):
            n = j - s.j0
            act.wait_ge(*s.summed.at(n + 1))
            if n >= 1:
                act.wait_ge(*s.stored.at(16 * n))
            dst = s.row[0:1, n % s.n_acc, :] if s.bias is None else s.row[0:1, :]
            for h in range(2):
                nc.scalar.activation(dst[:, h * BANK:(h + 1) * BANK], banks[h][0:1, :],
                                     ACT.Copy).then_inc(s.row_made.sem, 1)

        class Turn:
            def __init__(self, ready=None):
                self.ready = ready or Count("turn_ready", TT)
                self.turned = Count("turn_turned", 2 * TT)
                self.hi, self.lo = Count("turn_hi", 2 * TT), Count("turn_lo", 2 * TT)

        def turn_pe(pe, s, src, i):
            pe.wait_ge(*s.ready.at(i + 1))
            for h in range(2):
                n = 2 * i + h
                if n >= 4:
                    pe.wait_ge(*s.lo.at(n - 3))
                for q in range(4):
                    t = nc.tensor.transpose(bank[4 + n % 4][:, q * P:(q + 1) * P],
                                            src[:, (4 * h + q) * P:(4 * h + q + 1) * P], ident[:])
                t.then_inc(s.turned.sem, 1)

        def turn_act(act, s, dst_hi, i):
            for h in range(2):
                n = 2 * i + h
                act.wait_ge(*s.turned.at(n + 1))
                nc.scalar.activation(dst_hi[:, 4 * h:4 * h + 4, i * P:(i + 1) * P],
                                     bank[4 + n % 4][:].rearrange("p (k t) -> p k t", k=4),
                                     ACT.Copy).then_inc(s.hi.sem, 1)

        def turn_dve(dve, s, dst_hi, dst_lo, i):
            for h in range(2):
                n = 2 * i + h
                dve.wait_ge(*s.hi.at(n + 1))
                part = (slice(None), slice(4 * h, 4 * h + 4), slice(i * P, (i + 1) * P))
                nc.vector.tensor_tensor(dst_lo[part], bank[4 + n % 4][:].rearrange("p (k t) -> p k t", k=4),
                                        dst_hi[part].bitcast(F32), ALU.subtract).then_inc(s.lo.sem, 1)

        def modulate(dve, s, l, sc, sh, i):
            if i == 0:
                wait_row(dve, ("mod", l, sc))
                wait_row(dve, ("mod", l, sh))
            if i >= 2:
                dve.wait_ge(*s.turned.at(2 * (i - 1)))
            u = us[:, i % 2, :]
            m = nc.vector.scalar_tensor_tensor(out=u, in0=row(("mod", l, sc)), scalar=1.0, in1=xt[:, i, :],
                                               op0=ALU.add, op1=ALU.mult)
            link(dve, dve_n, dve_step, m)
            m = nc.vector.tensor_tensor(u, u, row(("mod", l, sh)), ALU.add).then_inc(s.ready.sem, 1)
            if i == TT - 1:
                dve.wait_ge(*s.ready.at(TT))
                dve.sem_inc(row_used, 2)

        class Norm:
            def __init__(self, l, w):
                self.l, self.w, self.gate = l, w, ("mod", l, (G1, G2)[w])
                (self.stat, self.root, self.coef, self.norm, self.gain, self.done) = (
                    Count("ln_" + n, TT) for n in ("stat", "root", "coef", "norm", "gain", "done"))

        def norm_stats(dve, s, i):
            for h in range(2):
                b = nc.vector.bn_stats(ln_stat[:, i, 6 * h:6 * h + 6], xt[:, i, h * BANK:(h + 1) * BANK])
                b.then_inc(dve_step, 1)
                dve_n[0] += 1
            dve.wait_ge(dve_step, dve_n[0])
            nc.vector.bn_aggr(ln_mv[:, i, 0:2], ln_stat[:, i, :].rearrange("p (a b) -> p a b", b=6)
                              ).then_inc(s.stat.sem, 1)

        def norm_root(act, s, i):
            act.wait_ge(*s.stat.at(i + 1))
            nc.scalar.activation(ln_mv[:, i, 2:3], ln_mv[:, i, 1:2], ACT.Sqrt, bias=eps_col[:, 0:1]
                                 ).then_inc(s.root.sem, 1)

        def norm_coef(dve, s, i):
            dve.wait_ge(*s.root.at(i + 1))
            link(dve, dve_n, dve_step, nc.vector.reciprocal(ln_mv[:, i, 3:4], ln_mv[:, i, 2:3]))
            nc.vector.tensor_scalar(ln_mv[:, i, 4:5], ln_mv[:, i, 0:1], ln_mv[:, i, 3:4], -1.0, ALU.mult,
                                    ALU.mult).then_inc(s.coef.sem, 1)

        def norm_apply(act, s, i):
            act.wait_ge(*s.coef.at(i + 1))
            nc.scalar.activation(xt[:, i, :], xt[:, i, :], ACT.Identity, bias=ln_mv[:, i, 4:5],
                                 scale=ln_mv[:, i, 3:4]).then_inc(s.norm.sem, 1)

        def norm_gain(dve, s, i):
            if i == 0:
                wait_row(dve, ("g", s.l, s.w))
            dve.wait_ge(*s.norm.at(i + 1))
            nc.vector.tensor_tensor(xt[:, i, :], xt[:, i, :], row(("g", s.l, s.w)), ALU.mult).then_inc(s.gain.sem, 1)
            if i == TT - 1:
                dve.wait_ge(*s.gain.at(TT))
                dve.sem_inc(row_used, 1)

        def norm_shifts(pool, s, next_rows=()):
            for i in range(TT):
                if i == TT - 1:
                    for key in next_rows:
                        row_load(pool, R[key])
                norm_shift(pool, s, i)

        def norm_shift(pool, s, i):
            if i == 0:
                wait_row(pool, ("b", s.l, s.w))
            pool.wait_ge(*s.gain.at(i + 1))
            nc.gpsimd.tensor_tensor(xt[:, i, :], xt[:, i, :], row(("b", s.l, s.w)), ALU.add).then_inc(s.done.sem, 1)
            if i == TT - 1:
                pool.wait_ge(*s.done.at(TT))
                pool.sem_inc(row_used, 1)

        norms = {(l, w): Norm(l, w) for l in range(DEPTH) for w in range(2)}
        turn_u, turn_moe0, turn_x, turn_q, turn_o, turn_moe1 = (
            Turn(), Turn(), Turn(norms[0, 1].done), Turn(), Turn(), Turn())

        class Proj:
            def __init__(self, tag, b0):
                self.b0, self.mm, self.res = b0, Count("proj_mm", 2 * (TT - 1)), Count("proj_gated", 2 * TT)

        def proj_pe(pe, s, b0, free):
            for n in range(2):
                for kh in range(2):
                    b = b0 + 2 * n + kh
                    pe.wait_ge(lo_done, b + 1)
                    if kh == 0:
                        free(n)
                    wh = w_hi[:, b % NSPLIT, :].rearrange("p (k n) -> p k n", k=4)
                    wl = w_lo[:, b % NRAW, :].rearrange("p (k n) -> p k n", k=4)
                    for i in range(TT):
                        for kk in range(4):
                            k = 4 * kh + kk
                            t = slice(i * P, (i + 1) * P)
                            m = mm3(bank[4 * n + i][:], v_hi[:, k, t], v_lo[:, k, t], wh[:, kk, :], wl[:, kk, :],
                                    start=(k == 0), stop=(k == KD - 1))
                        if kh == 1 and i < TT - 1:
                            m.then_inc(s.mm.sem, 1)
                    m.then_inc(blk_used, 1)

        def proj_residual(dve, s, ln, n, i):
            if n == 0 and i == 0:
                wait_row(dve, ln.gate)
            if i < TT - 1:
                dve.wait_ge(*s.mm.at((TT - 1) * n + i + 1))
            else:
                dve.wait_ge(blk_used, s.b0 + 2 * n + 2)
            g = n * TT + i
            h = slice(n * BANK, (n + 1) * BANK)
            y = us[:, g % 2, 0:BANK]
            link(dve, dve_n, dve_step,
                 nc.vector.tensor_tensor(y, bank[4 * n + i][:], row(ln.gate)[:, h], ALU.mult))
            nc.vector.scalar_tensor_tensor(out=xt[:, i, h], in0=xt[:, i, h], scalar=ALPHA, in1=y,
                                           op0=ALU.mult, op1=ALU.add).then_inc(s.res.sem, 1)

        conv_c, conv_z, conv_t, conv_v, conv_hi, conv_lo = (sem("conv_" + n) for n in ("c", "z", "t", "v", "hi", "lo"))
        cout = Proj("cout", B_COUT)
        N_CIN = len(conv_in)
        MACS_FIRST, MACS_SLOT = 16, 4

        def conv_product(eng, g, m):
            if m < 3:
                eng.wait_ge(conv_mm, 3 * g + m + 1)
            else:
                eng.wait_ge(blk_used, 2 * g + 2)

        def conv_pe(pe):
            for b in range(N_CIN):
                g, kh = b // 2, b % 2
                if b >= 3 and b % 2 == 1:
                    mod_sums(pe, ada_a, (b + 1) // 2, bank[4:6])
                pe.wait_ge(lo_done, b + 1)
                wh = w_hi[:, b % NSPLIT, :].rearrange("p (k n) -> p k n", k=4)
                wl = w_lo[:, b % NRAW, :].rearrange("p (k n) -> p k n", k=4)
                for m in range(4):
                    if kh == 0 and g >= 1:
                        pe.wait_ge((conv_c, conv_z, conv_v)[(g - 1) % 3], 4 * ((g - 1) // 3) + m + 1)
                    for kk in range(4):
                        k = 4 * kh + kk
                        c_ = slice(m * P, (m + 1) * P)
                        mm = mm3(bank[m][:], wh[:, kk, c_], wl[:, kk, c_], u_hi[:, k, :], u_lo[:, k, :],
                                 start=(k == 0), stop=(k == KD - 1))
                    if kh == 1 and m < 3:
                        mm.then_inc(conv_mm, 1)
                mm.then_inc(blk_used, 1)
            mod_sums(pe, ada_a, 7, bank[4:6])

            def free(n):
                if n == 0:
                    pe.wait_ge(conv_v, 2 * 4)
                    pe.wait_ge(conv_lo, 2 * 4)
                else:
                    pe.wait_ge(*ada_a.row_made.at(16))
            proj_pe(pe, cout, B_COUT, free)

        def conv_act(act):
            for b in range(N_CIN):
                g, kh = b // 2, b % 2
                half, part = g // 3, g % 3
                if kh == 1:
                    if part == 0:
                        for m in range(4):
                            conv_product(act, g, m)
                            if half:
                                act.wait_ge(conv_lo, m + 1)
                            else:
                                act.wait_ge(*turn_u.turned.at(2 * TT))
                            nc.scalar.activation(ct[:, m, :], bank[m][:], ACT.Copy).then_inc(conv_c, 1)
                    if part == 1:
                        for m in range(4):
                            q = 4 * half + m
                            act.wait_ge(conv_z, q + 1)
                            nc.scalar.activation(ct[:, m, :], z[:, m, 2:2 + SEQ], ACT.Identity,
                                                 bias=small[:, C_CB + q:C_CB + q + 1],
                                                 scale=small[:, C_CW + 16 + q:C_CW + 17 + q]).then_inc(conv_t, 1)
                    if part == 2:
                        for m in range(4):
                            q = 4 * half + m
                            act.wait_ge(conv_v, q + 1)
                            nc.scalar.activation(v_hi[:, q, :], ct[:, m, :], ACT.Copy).then_inc(conv_hi, 1)
                split_hi(act, b + NSPLIT)
                if b >= 3 and b % 2 == 1:
                    mod_rows(act, ada_a, (b + 1) // 2, bank[4:6])
                    mod_store(act, ada_a, (b + 1) // 2)
            mod_rows(act, ada_a, 7, bank[4:6])
            mod_store(act, ada_a, 7)

        def conv_dve(dve):
            for b in range(N_CIN):
                g, kh = b // 2, b % 2
                half, part = g // 3, g % 3
                if kh == 1 and part == 1:
                    for m in range(4):
                        q = 4 * half + m
                        conv_product(dve, g, m)
                        dve.wait_ge(conv_c, q + 1)
                        nc.vector.tensor_tensor(z[:, m, 2:2 + SEQ], ct[:, m, :], bank[m][:], ALU.mult
                                                ).then_inc(conv_z, 1)
                if kh == 1 and part == 2:
                    for m in range(4):
                        conv_product(dve, g, m)
                        nc.vector.tensor_tensor(ct[:, m, :], ct[:, m, :], bank[m][:], ALU.mult
                                                ).then_inc(conv_v, 1)
                split_lo(dve, b + NSPLIT)
                ada_macs(dve, ada_a, MACS_FIRST + MACS_SLOT * b, MACS_SLOT)
                if kh == 1 and part == 1:
                    for tap in (1, 0):
                        for m in range(4):
                            q = 4 * half + m
                            if tap == 1:
                                dve.wait_ge(conv_t, q + 1)
                            t = nc.vector.scalar_tensor_tensor(
                                out=ct[:, m, :], in0=z[:, m, tap:tap + SEQ],
                                scalar=small[:, C_CW + 8 * tap + q:C_CW + 8 * tap + q + 1], in1=ct[:, m, :],
                                op0=ALU.mult, op1=ALU.add)
                            t.then_inc(dve_step, 1)
                            dve_n[0] += 1
                        dve.wait_ge(dve_step, dve_n[0])
                if kh == 1 and part == 2:
                    for m in range(4):
                        q = 4 * half + m
                        dve.wait_ge(conv_hi, q + 1)
                        nc.vector.tensor_tensor(v_lo[:, q, :], ct[:, m, :], v_hi[:, q, :].bitcast(F32),
                                                ALU.subtract).then_inc(conv_lo, 1)

        def proj_norm_act(act, ln, b0):
            for b in range(b0, b0 + 3):
                split_hi(act, b + NSPLIT)
            for i in range(TT):
                norm_root(act, ln, i)
                norm_apply(act, ln, i)
            if b0 + 3 + NSPLIT < B_END:
                split_hi(act, b0 + 3 + NSPLIT)

        def proj_norm_dve(dve, s, ln, b0, times):
            split_lo(dve, b0 + NSPLIT)
            dve.wait_ge(x_back, 16 * TT * times)
            split_lo(dve, b0 + 1 + NSPLIT)
            for i in range(TT):
                proj_residual(dve, s, ln, 0, i)
            split_lo(dve, b0 + 2 + NSPLIT)
            for i in range(TT + 1):
                if i >= 1:
                    norm_coef(dve, ln, i - 1)
                if i < TT:
                    proj_residual(dve, s, ln, 1, i)
                    dve.wait_ge(*s.res.at(TT + i + 1))
                    norm_stats(dve, ln, i)
                if i == TT - 1:
                    dve.sem_inc(row_used, 1)
                if i >= 1:
                    norm_gain(dve, ln, i - 1)
            split_lo(dve, b0 + 3 + NSPLIT)

        PAIRS = NE // 2
        R0 = S0 + 24 * KB
        xg = at("xg", [P, 2, D], F32, V0)
        sg = at("sg", [P, FF], F32, V0 + 8 * KB)
        hh = at("hh", [P, FF], F32, V0 + 10 * KB)
        ye = at("ye", [P, 2, D], F32, V0 + 12 * KB)
        xe_hi = at("xe_hi", [P, 2, KD, P], F32R, S0)
        xe_lo = at("xe_lo", [P, 2, KD, P], F32R, S0 + 8 * KB)
        ht_hi = at("ht_hi", [P, 4, P], F32R, S0 + 16 * KB)
        ht_lo = at("ht_lo", [P, 4, P], F32R, S0 + 18 * KB)
        yg = at("yg", [P, 2 * TT, D], F32, U0)
        rat = [R0]

        def rnew(name, shape, dt=F32):
            n = 1
            for s in shape[1:]:
                n *= s
            here = rat[0]
            rat[0] += (n * (2 if dt == BF16 else 4) + 31) // 32 * 32
            assert rat[0] <= S0 + 32 * KB
            return at(name, shape, dt, here)

        rw = rnew("rw", [P, KD, NE])
        rw_hi = rnew("rw_hi", [P, KD, NE], F32R)
        rw_lo = rnew("rw_lo", [P, KD, NE], F32R)
        slots = rnew("slots", [P, P])
        dec16 = rnew("dec16", [P, NE])
        dec4 = rnew("dec4", [P, NG])
        base_e = rnew("base_e", [P, NE])
        rbias = rnew("rbias", [P, NE])
        tokc = rnew("tokc", [P, TT, 2], BF16)
        aff = rnew("aff", [P, TT, NE])
        bia = rnew("bia", [P, TT, NE])
        tmp = rnew("tmp", [P, TT, NE])
        oh1 = rnew("oh1", [P, TT, NE])
        oh2 = rnew("oh2", [P, TT, NE])
        pos = rnew("pos", [P, TT, NE])
        pairs = rnew("pairs", [P, TT * NG, 6])
        gs = rnew("gs", [P, TT, NG])
        ohg = rnew("ohg", [P, TT, NG])
        chosen = rnew("chosen", [P, TT, NE], BF16)
        col = rnew("col", [P, 8, TT])
        wk = rnew("wk", [P, 2, TT])
        posm = rnew("posm", [P, NE, TT])
        oneh = rnew("oneh", [P, 2, TT, P], BF16)
        place, base, prow, wpass = (rnew(n, [P, 2, TT]) for n in ("place", "base", "prow", "wpass"))
        longest = rnew("longest", [P, 1])
        yrow = rnew("yrow", [P, 2, TT], U32)
        tok = rnew("tok", [P, 2, 1], U32)
        longest_u = rnew("longest_u", [P, 1], U32)

        class Moe:
            def __init__(self, l):
                self.l, self.b0, self.ln = l, B_MOE[l], norms[l, 1]
                self.u, self.y = scratch[f"u{l}"], scratch[f"y{l}"]
                self.logit_copied, self.logit_turned = Count("moe_logit_copied", 1), Count("moe_logit_turned", 1)
                once = {n: Count("moe_" + n, 1) for n in ("consts", "rw_hi_made", "rw_lo_made", "logit", "exp_in",
                                                           "expd", "chose", "posd")}
                (self.consts, self.rw_hi_made, self.rw_lo_made, self.logit, self.exp_in, self.expd, self.chose,
                 self.posd) = once.values()
                self.rw_in, self.listed = Count("moe_rw_in", 32), Count("moe_listed", 3)
                self.over_done = Count("moe_over_done", 1)
                each = {n: Count("moe_" + n, NE) for n in (
                    "oh_made", "tok_mm", "tok_made", "xg_turned", "xe_hi_made", "xe_lo_made", "sg_made", "h_made",
                    "h_turned", "ht_hi_made", "ht_lo_made", "y_made")}
                (self.oh_made, self.tok_mm, self.tok_made, self.xg_turned, self.xe_hi_made, self.xe_lo_made,
                 self.sg_made, self.h_made, self.h_turned, self.ht_hi_made, self.ht_lo_made, self.y_made) = each.values()
                self.y_w1, self.res = Count("moe_y_w1", TT), Count("moe_res", TT)
                self.turn = (turn_moe0, turn_moe1)[l]
                self.u_out = [Count(f"moe_u_out{i}", 32) for i in range(2)]
                self.xg_in = [Count(f"moe_xg_in{i}", 8 * NE) for i in range(2)]
                self.y_out = [Count(f"moe_y_out{i}", 8 * NE) for i in range(2)]
                self.yg_in = [Count(f"moe_yg_in{i}", 32) for i in range(TT)]

        moes = [Moe(l) for l in range(DEPTH)]

        def bc(ap, shape, axis):
            return ap.unsqueeze(axis).to_broadcast(shape)

        def moe_consts(pool, s):
            def it(dst, pattern, base, mult):
                return nc.gpsimd.iota(dst, pattern=pattern, base=base, channel_multiplier=mult,
                                      allow_small_or_imprecise_dtypes=True)
            if s.l == 0:
                pool.wait_ge(*ada_a.stored.at(16 * 8))
            it(slots[:], [[1, P]], 0, 0)
            it(dec16[:], [[-1, NE]], NE, 0)
            it(dec4[:], [[-1, NG]], NG, 0)
            it(base_e[:], [[CAP, NE]], 0, 0)
            it(tokc[:, :, 0:1], [[0, TT], [0, 1]], 0, 1)
            it(tokc[:, :, 1:2], [[P, TT], [0, 1]], 0, 0).then_inc(s.consts.sem, 1)
            pool.dma_start(rw[:], router_w.rearrange("(k p) n -> p k n", p=P)).then_inc(s.rw_in.sem, 16)
            pool.dma_start(rbias[:], router_bias.partition_broadcast(P)).then_inc(s.rw_in.sem, 16)

        def router_pe(pe, s):
            pe.wait_ge(*s.rw_lo_made.at(1))
            pe.wait_ge(*s.turn.lo.at(2 * TT))
            for k in range(KD):
                m = mm3(bank[0][0:NE, :], rw_hi[:, k, :], rw_lo[:, k, :], u_hi[:, k, :], u_lo[:, k, :],
                        start=(k == 0), stop=(k == KD - 1))
            m.then_inc(s.logit.sem, 1)
            pe.wait_ge(*s.logit_copied.at(1))
            for i in range(TT):
                m = nc.tensor.transpose(bank[2][:, i * NE:(i + 1) * NE], sg[0:NE, i * P:(i + 1) * P],
                                        ident[0:NE, 0:NE])
            m.then_inc(s.logit_turned.sem, 1)

        def route_dve(dve, s):
            def go(ins):
                link(dve, dve_n, dve_step, ins)

            V = nc.vector
            full, grp = [P, TT, NE], [P, TT, NG]
            dve.wait_ge(*s.consts.at(1))
            dve.wait_ge(*s.logit_turned.at(1))
            lg = bank[2][:, 0:TT * NE].rearrange("p (i e) -> p i e", e=NE)
            go(V.tensor_reduce(col[:, 0, :], lg, AX_X, ALU.max))
            V.tensor_tensor(aff[:], lg, bc(col[:, 0, :], full, 2), ALU.subtract).then_inc(s.exp_in.sem, 1)
            dve.wait_ge(*s.expd.at(1))
            go(V.tensor_reduce(col[:, 1, :], aff[:], AX_X, ALU.add))
            go(V.reciprocal(col[:, 1, :], col[:, 1, :]))
            go(V.tensor_tensor(aff[:], aff[:], bc(col[:, 1, :], full, 2), ALU.mult))
            dve.wait_ge(*s.rw_in.at(32))
            go(V.tensor_tensor(bia[:], aff[:], bc(rbias[:], full, 1), ALU.add))
            b4 = bia[:].rearrange("p i (g e) -> p (i g) e", e=EPG)
            for at_, lo_, hi_ in ((0, (0, 3), (1, 4)), (3, (0, 2), (2, 4)), (5, (0, 1), (3, 4))):
                n = lo_[1] - lo_[0]
                m = V.tensor_tensor(pairs[:, :, at_:at_ + n], b4[:, :, lo_[0]:lo_[1]], b4[:, :, hi_[0]:hi_[1]], ALU.add)
            go(m)
            go(V.tensor_reduce(gs[:].rearrange("p i g -> p (i g)"), pairs[:], AX_X, ALU.max))

            def first_max(dst, src, dec, shape, c0):
                go(V.tensor_reduce(col[:, c0, :], src, AX_X, ALU.max))
                go(V.tensor_tensor(dst, src, bc(col[:, c0, :], shape, 2), ALU.is_equal))
                go(V.tensor_tensor(dst, dst, bc(dec, shape, 1), ALU.mult))
                go(V.tensor_reduce(col[:, c0, :], dst, AX_X, ALU.max))
                go(V.tensor_tensor(dst, dst, bc(col[:, c0, :], shape, 2), ALU.is_equal))

            first_max(ohg[:], gs[:], dec4[:], grp, 2)
            go(V.tensor_scalar(gs[:], ohg[:], 1.0, -NEG, ALU.subtract, ALU.mult))
            t4 = tmp[:].rearrange("p i (g e) -> p (i g) e", e=EPG)
            go(V.tensor_tensor(t4, b4, bc(gs[:].rearrange("p i g -> p (i g)"), [P, TT * NG, EPG], 2), ALU.add))
            first_max(oh1[:], tmp[:], dec16[:], full, 3)
            go(V.scalar_tensor_tensor(out=tmp[:], in0=oh1[:], scalar=2 * NEG, in1=tmp[:], op0=ALU.mult, op1=ALU.add))
            first_max(oh2[:], tmp[:], dec16[:], full, 4)
            V.tensor_tensor(chosen[:], oh1[:], oh2[:], ALU.add).then_inc(s.chose.sem, 1)
            for k, oh in enumerate((oh1, oh2)):
                go(V.tensor_tensor(tmp[:], aff[:], oh[:], ALU.mult))
                go(V.tensor_reduce(col[:, 5 + k, :], tmp[:], AX_X, ALU.add))
            go(V.tensor_tensor(col[:, 7, :], col[:, 5, :], col[:, 6, :], ALU.add))
            go(V.reciprocal(col[:, 7, :], col[:, 7, :]))
            for k in range(2):
                go(V.tensor_tensor(wk[:, k, :], col[:, 5 + k, :], col[:, 7, :], ALU.mult))
            dve.wait_ge(*s.posd.at(1))
            go(V.tensor_copy(pos[:], bank[1][:, 0:TT * NE].rearrange("p (i e) -> p i e", e=NE)))
            go(V.tensor_scalar(tmp[:], chosen[:], -4096.0, 4096.0, ALU.mult, ALU.add))
            V.tensor_tensor(posm[:, 0:NE, :].rearrange("p e i -> p i e"), tmp[:], pos[:], ALU.add).then_inc(s.listed.sem, 1)
            for k, oh in enumerate((oh1, oh2)):
                dve.wait_ge(*s.listed.at(1))
                go(V.tensor_tensor(tmp[:], pos[:], oh[:], ALU.mult))
                go(V.tensor_reduce(place[:, k, :], tmp[:], AX_X, ALU.add))
                go(V.tensor_tensor(tmp[:], bc(base_e[:], full, 1), oh[:], ALU.mult))
                go(V.tensor_reduce(base[:, k, :], tmp[:], AX_X, ALU.add))
            pass_rows(dve)
            V.tensor_reduce(longest[:], bank[1][:, TT * NE:(TT + 1) * NE], AX_X, ALU.max).then_inc(s.listed.sem, 1)
            dve.wait_ge(*s.listed.at(2))
            V.tensor_copy(longest_u[:], longest[:]).then_inc(s.listed.sem, 1)

        def pass_rows(dve):
            def go(ins):
                link(dve, dve_n, dve_step, ins)
            V = nc.vector
            go(V.tensor_scalar(prow[:], place[:], 0.0, float(CAP - 1), ALU.max, ALU.min))
            go(V.tensor_tensor(yrow[:], prow[:], base[:], ALU.add))
            go(V.tensor_scalar(prow[:], place[:], 0.0, None, ALU.is_ge))
            go(V.scalar_tensor_tensor(out=prow[:], in0=place[:], scalar=float(LIMIT - 1), in1=prow[:], op0=ALU.is_le,
                                      op1=ALU.mult))
            go(V.tensor_tensor(wpass[:], prow[:], wk[:], ALU.mult))

        def places_pe(pe, s):
            pe.wait_ge(*s.chose.at(1))
            for i in range(TT + 1):
                o = bank[1][:, i * NE:(i + 1) * NE]
                for q in range(min(i + 1, TT)):
                    m = nc.tensor.matmul(o, ones_b[:] if q < i else before_b[:], chosen[:, q, :], start=(q == 0),
                                         stop=(q == min(i, TT - 1)))
            m.then_inc(s.posd.sem, 1)

        def after(eng, semaphore, value):
            if not isinstance(value, int) or value > 0:
                if isinstance(semaphore, Count):
                    semaphore, value = semaphore.at(value)
                eng.wait_ge(semaphore, value)

        def one_hot(dve, s, pair, p):
            after(dve, s.tok_mm, 2 * pair + p - 1)
            shape = [P, TT, P]
            nc.vector.tensor_tensor(oneh[:, p, :, :], bc(slots[:], shape, 1),
                                    bc(posm[:, 2 * pair + p, :], shape, 2), ALU.is_equal).then_inc(s.oh_made.sem, 1)

        def list_pe(pe, s, pair, p):
            pe.wait_ge(*s.oh_made.at(2 * pair + p + 1))
            after(pe, s.tok_made, 2 * pair + p)
            for i in range(TT):
                m = nc.tensor.matmul(bank[7][:, 0:2], oneh[:, p, i, :], tokc[:, i, :], start=(i == 0),
                                     stop=(i == TT - 1))
            m.then_inc(s.tok_mm.sem, 1)

        def list_dve(dve, s, pair, p):
            dve.wait_ge(*s.tok_mm.at(2 * pair + p + 1))
            after(dve, s.xg_in[p], 16 * pair)
            nc.vector.tensor_scalar(tok[:, p, :], bank[7][:, 0:1], bank[7][:, 1:2], None, ALU.add).then_inc(s.tok_made.sem, 1)

        def gather(pool, s, pair, p):
            pool.wait_ge(*s.tok_made.at(2 * pair + p + 1))
            after(pool, s.xg_turned, 2 * pair + p - 1)
            pool.indirect_dma_start(out=xg[:, p, :], out_offset=None, in_=s.u[:, :],
                                    in_offset=bass.IndirectOffsetOnAxis(ap=tok[:, p, :], axis=0)
                                    ).then_inc(s.xg_in[p].sem, 16)

        def rows_pe(pe, s, pair, p):
            pe.wait_ge(*s.xg_in[p].at(16 * pair + 16))
            after(pe, s.xe_lo_made, 2 * pair + p)
            after(pe, s.ht_lo_made, 2 * pair + p - 1)
            pe.wait_ge(*s.tok_made.at(2 * pair + p + 1))
            for k in range(KD):
                m = nc.tensor.transpose(bank[6 + k // 4][:, (k % 4) * P:(k % 4 + 1) * P],
                                        xg[:, p, k * P:(k + 1) * P], ident[:])
            m.then_inc(s.xg_turned.sem, 1)

        def rows_act(act, s, pair, p):
            act.wait_ge(*s.xg_turned.at(2 * pair + p + 1))
            if not isinstance(pair, int) or pair >= 1:
                act.wait_ge(blk_used, s.b0 + EBLK * (2 * pair + p - 2) + 4)
            for h in range(2):
                m = nc.scalar.activation(xe_hi[:, p, 4 * h:4 * h + 4, :],
                                         bank[6 + h][:].rearrange("p (k t) -> p k t", k=4), ACT.Copy)
            m.then_inc(s.xe_hi_made.sem, 1)

        def rows_dve(dve, s, pair, p):
            dve.wait_ge(*s.xe_hi_made.at(2 * pair + p + 1))
            for h in range(2):
                m = nc.vector.tensor_tensor(xe_lo[:, p, 4 * h:4 * h + 4, :],
                                            bank[6 + h][:].rearrange("p (k t) -> p k t", k=4),
                                            xe_hi[:, p, 4 * h:4 * h + 4, :].bitcast(F32), ALU.subtract)
            m.then_inc(s.xe_lo_made.sem, 1)

        def step_block(s, pair, p, i):
            first = s.b0 + 2 + EBLK * p + i
            return (first + 2 * EBLK * pair, first % NRAW, first // NRAW + 2 * EBLK // NRAW * pair,
                    first % NSPLIT)

        def load_part(sp, s, pair, p, i, matrix, e, j):
            b, slot, _, _ = step_block(s, pair, p, i)
            sp.wait_ge(blk_used, b - NRAW + 1)
            sp.dma_start(raw[:, slot, :].rearrange("p (k n) -> p k n", k=2),
                         matrix[s.l, e, j * 2 * P:(j + 1) * 2 * P, :].rearrange("(k p) n -> p k n", p=P)
                         ).then_inc(raw_in[slot], 16)

        def step_load(sp, s, pair, p, first=0, last=False):
            e = 2 * pair + p
            parts = [(w_gu, e, 2), (w_gu, e, 3)]
            if not last:
                parts += [(w_gu, e + 1, 0), (w_gu, e + 1, 1)]
            parts += [(w_down, e, 0), (w_down, e, 1)]
            for i, part in enumerate(parts):
                if i >= first:
                    load_part(sp, s, pair, p, i, *part)

        def step_hi(act, s, pair, p, i):
            b, slot, used, hslot = step_block(s, pair, p, i)
            if not isinstance(b, int) or b < B_END:
                act.wait_ge(raw_in[slot], 16 * used + 16)
                act.wait_ge(blk_used, b - NSPLIT + 1)
                nc.scalar.activation(w_hi[:, hslot, :], raw[:, slot, :], ACT.Copy).then_inc(hi_done, 1)

        def step_lo(dve, s, pair, p, i):
            b, slot, _, hslot = step_block(s, pair, p, i)
            if not isinstance(b, int) or b < B_END:
                dve.wait_ge(hi_done, b + 1)
                nc.vector.tensor_tensor(w_lo[:, slot, :], raw[:, slot, :], w_hi[:, hslot, :].bitcast(F32),
                                        ALU.subtract).then_inc(lo_done, 1)

        def gate_up(pe, s, pair, p, i, q, j):
            b, slot, _, hslot = step_block(s, pair, p, i)
            pe.wait_ge(lo_done, b + 1)
            for kk in range(2):
                k = 2 * j + kk
                for h in range(2):
                    c_ = slice(kk * D + h * FF, kk * D + (h + 1) * FF)
                    m = mm3(bank[2 * q + h][:], xe_hi[:, q, k, :], xe_lo[:, q, k, :], w_hi[:, hslot, c_],
                            w_lo[:, slot, c_], start=(k == 0), stop=(k == KD - 1))
            m.then_inc(blk_used, 1)

        def expert_pe(pe, s, pair, p, last=False):
            e, q = 2 * pair + p, 1 - p
            gate_up(pe, s, pair, p, 0, p, 2)
            if not last:
                rows_pe(pe, s, pair + p, q)
            gate_up(pe, s, pair, p, 1, p, 3)
            if not last:
                pe.wait_ge(*s.xe_lo_made.at(e + 2))
                after(pe, s.h_made, e)
                gate_up(pe, s, pair, p, 2, q, 0)
            if not (isinstance(pair, int) and pair == PAIRS - 1):
                list_pe(pe, s, pair + 1, p)
            pe.wait_ge(*s.h_made.at(e + 1))
            for k in range(4):
                m = nc.tensor.transpose(bank[6][:, k * P:(k + 1) * P], hh[:, k * P:(k + 1) * P], ident[:])
            m.then_inc(s.h_turned.sem, 1)
            if not last:
                gate_up(pe, s, pair, p, 3, q, 1)
            pe.wait_ge(*s.ht_lo_made.at(e + 1))
            after(pe, s.y_made, e)
            for j in range(2):
                b, slot, _, hslot = step_block(s, pair, p, j + (2 if last else 4))
                pe.wait_ge(lo_done, b + 1)
                for kk in range(2):
                    k = 2 * j + kk
                    for h in range(2):
                        c_ = slice(kk * D + h * BANK, kk * D + (h + 1) * BANK)
                        m = mm3(bank[4 + h][:], ht_hi[:, k, :], ht_lo[:, k, :], w_hi[:, hslot, c_], w_lo[:, slot, c_],
                                start=(k == 0), stop=(k == 3))
                m.then_inc(blk_used, 1)

        def expert_act(act, s, pair, p, last=False):
            e = 2 * pair + p
            if not last:
                rows_act(act, s, pair + p, 1 - p)
            step_hi(act, s, pair, p, 3)
            act.wait_ge(blk_used, s.b0 + EBLK * e + 4)
            after(act, s.h_made, e)
            nc.scalar.activation(sg[:], bank[2 * p][:], ACT.Silu).then_inc(s.sg_made.sem, 1)
            if not last:
                step_hi(act, s, pair, p, 4)
            act.wait_ge(*s.h_turned.at(e + 1))
            nc.scalar.activation(ht_hi[:], bank[6][:].rearrange("p (k t) -> p k t", k=4), ACT.Copy
                                 ).then_inc(s.ht_hi_made.sem, 1)
            for i in range(5, 9) if not last else (4,):
                step_hi(act, s, pair, p, i)
            act.wait_ge(blk_used, s.b0 + EBLK * (e + 1) + (0 if last else 2))
            after(act, s.y_out[p], 16 * pair)
            for h in range(2):
                m = nc.scalar.activation(ye[:, p, h * BANK:(h + 1) * BANK], bank[4 + h][:], ACT.Copy)
            m.then_inc(s.y_made.sem, 1)
            act.wait_ge(*s.y_made.at(e + 1))
            act.dma_start(s.y.rearrange("(e t) d -> e t d", t=CAP)[e], ye[:, p, :]).then_inc(s.y_out[p].sem, 16)
            if last:
                step_hi(act, s, pair, p, 5)
                step_hi(act, s, pair, p, 6)

        def expert_dve(dve, s, pair, p, last=False):
            e = 2 * pair + p
            if not (isinstance(pair, int) and pair == PAIRS - 1):
                one_hot(dve, s, pair + 1, p)
            if not last:
                rows_dve(dve, s, pair + p, 1 - p)
            step_lo(dve, s, pair, p, 3)
            dve.wait_ge(*s.sg_made.at(e + 1))
            after(dve, s.h_turned, e)
            nc.vector.tensor_tensor(hh[:], sg[:], bank[2 * p + 1][:], ALU.mult).then_inc(s.h_made.sem, 1)
            if not last:
                step_lo(dve, s, pair, p, 4)
            dve.wait_ge(*s.ht_hi_made.at(e + 1))
            nc.vector.tensor_tensor(ht_lo[:], bank[6][:].rearrange("p (k t) -> p k t", k=4),
                                    ht_hi[:].bitcast(F32), ALU.subtract).then_inc(s.ht_lo_made.sem, 1)
            if not (isinstance(pair, int) and pair == PAIRS - 1):
                list_dve(dve, s, pair + 1, p)
            for i in range(5, 9) if not last else range(4, 7):
                step_lo(dve, s, pair, p, i)

        def begin_pe(pe, s):
            pe.wait_ge(*s.xe_lo_made.at(1))
            gate_up(pe, s, 0, 0, -2, 0, 0)
            gate_up(pe, s, 0, 0, -1, 0, 1)

        def begin_act(act, s):
            step_hi(act, s, 0, 0, 1)
            step_hi(act, s, 0, 0, 2)

        def begin_dve(dve, s):
            step_lo(dve, s, 0, 0, 1)
            step_lo(dve, s, 0, 0, 2)

        def all_experts(eng, body, s):
            body(eng, s, 0, 0)
            body(eng, s, 0, 1)
            with eng.Fori(1, PAIRS - 1) as pair:
                body(eng, s, pair, 0)
                body(eng, s, pair, 1)
            body(eng, s, PAIRS - 1, 0)
            body(eng, s, PAIRS - 1, 1, last=True)


        over_w = at("over_w", [P, KD, D], F32, V0)
        over_wd = at("over_wd", [P, 4, D], F32, S0)
        over_ht = at("over_ht", [P, 4, P], F32, S0 + 16 * KB)
        over_sg = at("over_sg", [P, FF], F32, S0 + 18 * KB)
        over_h = at("over_h", [P, FF], F32, S0 + 20 * KB)
        over_y = at("over_y", [P, TT, D], F32, U0)
        over_u = at("over_u", [P, KD, SEQ], F32, U0 + 16 * KB)
        over_k = at("over_k", [P, NE, TT], F32, S0 + 22 * KB)
        over_tmp = at("over_tmp", [P, TT, NE], F32, S0 + 22 * KB + 512)

        class Over:
            def __init__(self, l):
                (self.weights_in, self.gate_up, self.silu, self.h, self.turned, self.ht, self.down,
                 self.added, self.step) = (
                    sem(f"over{l}_" + n) for n in ("weights_in", "gate_up", "silu", "h", "turned", "ht",
                                                   "down", "added", "step"))

        overs = [Over(l) for l in range(DEPTH)]

        def if_over(eng, s):
            eng.wait_ge(*s.listed.at(3))
            return eng.If(eng.value_load(longest_u[0:1, 0:1], min_val=0, max_val=SEQ) > LIMIT)

        def over_load(sp, s, o, e):
            sp.dma_start(over_w[:], w_gu[s.l, e].rearrange("(k p) n -> p k n", p=P)).then_inc(o.weights_in, 16)
            sp.dma_start(over_wd[:], w_down[s.l, e].rearrange("(k p) n -> p k n", p=P)).then_inc(o.weights_in, 16)

        def over_sp(sp, s):
            o = overs[s.l]
            with if_over(sp, s):
                for p in range(2):
                    sp.wait_ge(*s.y_out[p].at(16 * PAIRS))
                sp.wait_ge(blk_used, s.b0 + EBLK * NE)
                over_load(sp, s, o, 0)
                with sp.Fori(1, NE) as e:
                    sp.wait_ge(o.down, TT * e)
                    over_load(sp, s, o, e)

        def over_pe(pe, s):
            o = overs[s.l]
            with if_over(pe, s):
                pe.wait_ge(*s.y_made.at(NE))
                with pe.Fori(0, NE) as e:
                    pe.wait_ge(o.weights_in, 32 * e + 32)
                    for i in range(TT):
                        pe.wait_ge(o.added, TT * e + i + 1)
                        for k in range(KD):
                            for h in range(2):
                                m = nc.tensor.matmul(bank[h][:], over_u[:, k, i * P:(i + 1) * P],
                                                     over_w[:, k, h * FF:(h + 1) * FF], start=(k == 0),
                                                     stop=(k == KD - 1))
                        m.then_inc(o.gate_up, 1)
                        pe.wait_ge(o.h, TT * e + i + 1)
                        for k in range(4):
                            m = nc.tensor.transpose(bank[6][:, k * P:(k + 1) * P], over_h[:, k * P:(k + 1) * P],
                                                    ident[:])
                        m.then_inc(o.turned, 1)
                        pe.wait_ge(o.ht, TT * e + i + 1)
                        for k in range(4):
                            for h in range(2):
                                m = nc.tensor.matmul(bank[2 + h][:], over_ht[:, k, :],
                                                     over_wd[:, k, h * BANK:(h + 1) * BANK], start=(k == 0),
                                                     stop=(k == 3))
                        m.then_inc(o.down, 1)

        def over_act(act, s):
            o = overs[s.l]
            with if_over(act, s):
                with act.Fori(0, NE) as e:
                    for i in range(TT):
                        act.wait_ge(o.gate_up, TT * e + i + 1)
                        nc.scalar.activation(over_sg[:], bank[0][:], ACT.Silu).then_inc(o.silu, 1)
                        act.wait_ge(o.turned, TT * e + i + 1)
                        nc.scalar.activation(over_ht[:], bank[6][:].rearrange("p (k t) -> p k t", k=4), ACT.Copy
                                             ).then_inc(o.ht, 1)

        def over_dve(dve, s):
            o, n = overs[s.l], [0]

            def go(ins):
                link(dve, n, o.step, ins)

            V = nc.vector
            with if_over(dve, s):
                dve.wait_ge(blk_used, s.b0 + EBLK * NE)
                go(V.tensor_tensor(over_u[:], u_hi[:].bitcast(F32), u_lo[:].bitcast(F32), ALU.add))
                go(V.tensor_tensor(prow[:], wk[:], wpass[:], ALU.subtract))
                over_k_view = over_k[:].rearrange("p e i -> p i e")
                go(V.tensor_tensor(over_k_view, oh1[:], bc(prow[:, 0, :], [P, TT, NE], 2), ALU.mult))
                go(V.tensor_tensor(over_tmp[:], oh2[:], bc(prow[:, 1, :], [P, TT, NE], 2), ALU.mult))
                go(V.tensor_tensor(over_k_view, over_k_view, over_tmp[:], ALU.add))
                V.memset(over_y[:], 0.0).then_inc(o.added, 1)
                with dve.Fori(0, NE) as e:
                    for i in range(TT):
                        dve.wait_ge(o.silu, TT * e + i + 1)
                        V.tensor_tensor(over_h[:], over_sg[:], bank[1][:], ALU.mult).then_inc(o.h, 1)
                        dve.wait_ge(o.down, TT * e + i + 1)
                        dve.wait_ge(o.added, TT * e + i + 1)
                        for h in range(2):
                            y = over_y[:, i, h * BANK:(h + 1) * BANK]
                            m = V.scalar_tensor_tensor(out=y, in0=bank[2 + h][:], scalar=over_k[:, e, i:i + 1], in1=y,
                                                       op0=ALU.mult, op1=ALU.add)
                        m.then_inc(o.added, 1)
                dve.wait_ge(o.added, TT * NE + 1)
                wait_row(dve, s.ln.gate)
                for i in range(TT):
                    go(V.tensor_tensor(over_y[:, i, :], over_y[:, i, :], row(s.ln.gate), ALU.mult))
                    go(V.scalar_tensor_tensor(out=xt[:, i, :], in0=over_y[:, i, :], scalar=1.0 / ALPHA,
                                              in1=xt[:, i, :], op0=ALU.mult, op1=ALU.add))
            dve.sem_inc(s.over_done.sem, 1)
        def moe_sp(sp, s, next_blocks):
            load_part(sp, s, 0, 0, -2, w_gu, 0, 0)
            load_part(sp, s, 0, 0, -1, w_gu, 0, 1)
            load_part(sp, s, 0, 0, 0, w_gu, 0, 2)
            load_part(sp, s, 0, 0, 1, w_gu, 0, 3)
            load_part(sp, s, 0, 0, 2, w_gu, 1, 0)
            load_part(sp, s, 0, 0, 3, w_gu, 1, 1)
            for i in range(TT):
                sp.wait_ge(*s.turn.ready.at(i + 1))
                sp.dma_start(s.u[i * P:(i + 1) * P, :], us[:, i % 2, :]).then_inc(s.u_out[i % 2].sem, 16)
            step_load(sp, s, 0, 0, first=4)
            step_load(sp, s, 0, 1)
            with sp.Fori(1, PAIRS - 1) as pair:
                step_load(sp, s, pair, 0)
                step_load(sp, s, pair, 1)
            step_load(sp, s, PAIRS - 1, 0)
            step_load(sp, s, PAIRS - 1, 1, last=True)
            for b, src in next_blocks:
                load_block(sp, b, src)
            over_sp(sp, s)

        def moe_pool(pool, s):
            moe_consts(pool, s)
            row_load(pool, R[("mod", s.l, G2)])
            for p in range(2):
                pool.wait_ge(*s.u_out[p].at(32))
            for e in range(NE):
                gather(pool, s, e // 2, e % 2)
            row_load(pool, R[("g", s.l, 1)])
            row_load(pool, R[("b", s.l, 1)])
            for p in range(2):
                pool.wait_ge(*s.y_out[p].at(16 * PAIRS))
            pool.wait_ge(*s.listed.at(2))
            pool.wait_ge(*s.over_done.at(1))
            for i in range(TT):
                for k in range(2):
                    pool.indirect_dma_start(out=yg[:, 2 * i + k, :], out_offset=None, in_=s.y[:, :],
                                            in_offset=bass.IndirectOffsetOnAxis(ap=yrow[:, k, i:i + 1], axis=0)
                                            ).then_inc(s.yg_in[i].sem, 16)
            norm_shifts(pool, s.ln, [("mod", 1, SC1), ("mod", 1, SH1)] if s.l == 0 else [])

        def moe_act(act, s):
            act.wait_ge(*s.rw_in.at(32))
            nc.scalar.activation(rw_hi[:], rw[:], ACT.Copy).then_inc(s.rw_hi_made.sem, 1)
            for i in range(TT):
                turn_act(act, s.turn, u_hi, i)
            act.wait_ge(*s.logit.at(1))
            nc.scalar.activation(sg[0:NE, :], bank[0][0:NE, :], ACT.Copy).then_inc(s.logit_copied.sem, 1)
            act.wait_ge(*s.exp_in.at(1))
            nc.scalar.activation(aff[:], aff[:], ACT.Exp).then_inc(s.expd.sem, 1)
            rows_act(act, s, 0, 0)
            begin_act(act, s)
            all_experts(act, expert_act, s)
            over_act(act, s)
            for i in range(TT):
                act.wait_ge(*s.yg_in[i].at(32))
                nc.scalar.activation(yg[:, 2 * i, :], yg[:, 2 * i, :], ACT.Copy, scale=wpass[:, 0, i:i + 1]
                                     ).then_inc(s.y_w1.sem, 1)
                if i >= 1:
                    norm_root(act, s.ln, i - 1)
                    norm_apply(act, s.ln, i - 1)
            norm_root(act, s.ln, TT - 1)
            norm_apply(act, s.ln, TT - 1)

        def moe_dve(dve, s):
            dve.wait_ge(*s.rw_hi_made.at(1))
            nc.vector.tensor_tensor(rw_lo[:], rw[:], rw_hi[:].bitcast(F32), ALU.subtract).then_inc(s.rw_lo_made.sem, 1)
            for i in range(TT + 1):
                if i < TT:
                    dve.wait_ge(*norms[s.l, 0].done.at(i + 1))
                    if i >= 2:
                        dve.wait_ge(*s.u_out[i % 2].at(16))
                    modulate(dve, s.turn, s.l, SC2, SH2, i)
                if i >= 1:
                    turn_dve(dve, s.turn, u_hi, u_lo, i - 1)
            route_dve(dve, s)
            one_hot(dve, s, 0, 0)
            one_hot(dve, s, 0, 1)
            list_dve(dve, s, 0, 0)
            list_dve(dve, s, 0, 1)
            rows_dve(dve, s, 0, 0)
            begin_dve(dve, s)
            all_experts(dve, expert_dve, s)
            over_dve(dve, s)
            for i in range(TT + 1):
                if i >= 1:
                    norm_coef(dve, s.ln, i - 1)
                if i < TT:
                    if i == 0:
                        wait_row(dve, s.ln.gate)
                    dve.wait_ge(*s.y_w1.at(i + 1))
                    y = yg[:, 2 * i, :]
                    link(dve, dve_n, dve_step, nc.vector.scalar_tensor_tensor(
                        out=y, in0=yg[:, 2 * i + 1, :], scalar=wpass[:, 1, i:i + 1], in1=y, op0=ALU.mult, op1=ALU.add))
                    link(dve, dve_n, dve_step, nc.vector.tensor_tensor(y, y, row(s.ln.gate), ALU.mult))
                    nc.vector.scalar_tensor_tensor(out=xt[:, i, :], in0=xt[:, i, :], scalar=ALPHA, in1=y,
                                                   op0=ALU.mult, op1=ALU.add).then_inc(s.res.sem, 1)
                    dve.wait_ge(*s.res.at(i + 1))
                    norm_stats(dve, s.ln, i)
                if i == TT - 1:
                    dve.sem_inc(row_used, 1)
                if i >= 1:
                    norm_gain(dve, s.ln, i - 1)

        def moe_pe(pe, s):
            for i in range(TT):
                turn_pe(pe, s.turn, us[:, i % 2, :], i)
            router_pe(pe, s)
            places_pe(pe, s)
            list_pe(pe, s, 0, 0)
            list_pe(pe, s, 0, 1)
            pe.wait_ge(*s.turn.lo.at(2 * TT))
            pe.wait_ge(*s.tok_made.at(2))
            rows_pe(pe, s, 0, 0)
            begin_pe(pe, s)
            all_experts(pe, expert_pe, s)
            over_pe(pe, s)

        SEL, WIN = 0, 1
        HC = 2
        NC4 = NKV * NCMP
        VW = HD + 1
        vsw = at("vsw", [P, 2, TT, NKV, VW], F32, S0)
        S1 = S0 + (2 * TT * NKV * VW * 4 + 31) // 32 * 32
        kct = at("kct", [P, 4, SEQ], F32, S1)
        fl = at("fl", [P, 16, NC4], F32, S1 + 8 * KB)
        fl_lo = at("fl_lo", [P, 16, NC4], F32R, S1 + 8 * KB)
        fl_hi = at("fl_hi", [P, 16, NC4], F32R, S1 + 16 * KB)
        q2 = at("q2", [P, NH, SEQ], F32R, S1)
        k2_hi = at("k2_hi", [P, 2, NKV, SEQ], F32R, V0)
        k2_lo = at("k2_lo", [P, 2, NKV, SEQ], F32R, V0 + 16 * KB)
        w2 = at("w2", [P, 2, HC, HD], F32, U0)
        h1 = at("h1", [P, 2, HC, NC4], F32, U0 + KB)
        kcf = at("kcf", [P, NC4], F32, U0 + 4 * KB)
        wg = at("wg", [P, KD, 3 * NH], F32, S1 + 8 * KB)
        wg_hi = at("wg_hi", [P, KD, 3 * NH], F32R, S1 + 10 * KB)
        gate_t = at("gate_t", [P, SEQ], F32, S1 + 14 * KB)
        wg_lo = at("wg_lo", [P, KD, 3 * NH], F32R, S1 + 12 * KB)
        o_tok = at("o_tok", [P, TT, D], F32, U0)
        prob = at("prob", [P, 2, 2, SEQ], F32, U0 + 16 * KB)
        prob_t = at("prob_t", [P, 2, 2, SEQ], F32, U0 + 24 * KB)
        aat = [A0]

        def anew(name, shape, dt=F32):
            n = 1
            for s in shape[1:]:
                n *= s
            here = aat[0]
            aat[0] += (n * (2 if dt == BF16 else 4) + 31) // 32 * 32
            return at(name, shape, dt, here)

        kc2_hi = anew("kc2_hi", [P, NKV, 32], F32R)
        kc2_lo = anew("kc2_lo", [P, NKV, 32], F32R)
        vc = anew("vc", [P, NKV, VW])
        causal = anew("causal", [P, P], BF16)
        causal_c = anew("causal_c", [P, TT, 32], BF16)
        gates = anew("gates", [P, TT, NH, 3])
        bg = anew("bg", [P, 3 * NH])
        has_c = anew("has_c", [P, 1])
        snm = anew("snm", [P, 2, 2])
        cmax = anew("cmax", [P, TT])
        orec = anew("orec", [P, 2, 3])
        assert aat[0] <= A0 + 4 * KB
        prob_ct = at("prob_ct", [P, 2, SEQ], F32, A0 + 4 * KB)
        prob_c = at("prob_c", [P, 2, TT, 32], F32, A0 + 8 * KB)
        otmp = at("otmp", [P, 2, 3, HD], F32, A0 + 10 * KB)
        vb2 = at("vb2", [P, HD], F32, U0 + 5 * KB)

        kv_mm, kv_copy, kv_khi, kv_klo, kv_v = (sem("kv_" + n) for n in ("mm", "copy", "khi", "klo", "v"))
        fl_made, fl_hi_made, fl_lo_made = sem("fl_made"), sem("fl_hi"), sem("fl_lo")
        att_in, att_const = sem("att_in"), sem("att_const")
        gelu_made, kc_mm, kcf_made, kc_hi_made, kc_made = (sem(n) for n in ("gelu_made", "kc_mm", "kcf_made",
                                                                            "kc_hi_made", "kc_made"))
        wg_in, wg_hi_made, wg_lo_made, gate_mm, gate_sum, gate_sig, gate_made = (
            sem(n) for n in ("wg_in", "wg_hi_made", "wg_lo_made", "gate_mm", "gate_sum", "gate_sig", "gate_made"))
        gate_copied, gate_turned = sem("gate_copied"), sem("gate_turned")
        q_mm, q_hi, q_lo = sem("q_mm"), sem("q_hi"), sem("q_lo")
        x_saved = sem("x_saved")

        def kv_pe(pe):
            for i in range(TT):
                turn_pe(pe, turn_x, xt[:, i, :], i)
            pe.wait_ge(*turn_x.lo.at(2 * TT))
            kbanks, vbanks = {1: (4, 5), 2: (2, 3)}, {1: (6, 7, 0, 1), 2: (4, 5, 6, 7)}
            for g in range(3):
                for kh in range(2):
                    b = B_KV + 2 * g + kh
                    pe.wait_ge(lo_done, b + 1)
                    wh = w_hi[:, b % NSPLIT, :].rearrange("p (k n) -> p k n", k=4)
                    wl = w_lo[:, b % NRAW, :].rearrange("p (k n) -> p k n", k=4)
                    for m in range(4 if g == 0 else 2):
                        if kh == 0 and g == 2 and m == 0:
                            pe.wait_ge(kv_copy, 4)
                        for kk in range(4):
                            k = 4 * kh + kk
                            c_ = slice(m * P, (m + 1) * P)
                            o = bank[m if g == 0 else kbanks[g][m]][:]
                            mm = mm3(o, wh[:, kk, c_], wl[:, kk, c_], u_hi[:, k, :], u_lo[:, k, :],
                                     start=(k == 0), stop=(k == KD - 1))
                        if kh == 1 and not (g == 0 and m == 3):
                            mm.then_inc(kv_mm, 1)
                    if g:
                        for i in range(TT):
                            if kh == 0 and g == 1 and i == 2:
                                pe.wait_ge(kv_copy, 2)
                            if kh == 0 and g == 2 and i == 0:
                                pe.wait_ge(kv_klo, 4)
                            if kh == 0 and g == 2 and i == 2:
                                pe.wait_ge(kv_v, 1 + 2)
                            for kk in range(4):
                                k = 4 * kh + kk
                                t = slice(i * P, (i + 1) * P)
                                mm = mm3(bank[vbanks[g][i]][:, 0:2 * P], u_hi[:, k, t], u_lo[:, k, t],
                                         wh[:, kk, 2 * P:4 * P], wl[:, kk, 2 * P:4 * P], start=(k == 0),
                                         stop=(k == KD - 1))
                            if kh == 1 and i < TT - 1:
                                mm.then_inc(kv_mm, 1)
                    mm.then_inc(blk_used, 1)

        def kv_act(act):
            for i in range(TT):
                turn_act(act, turn_x, u_hi, i)
            for g in range(3):
                split_hi(act, B_KV + 2 * g + NSPLIT)
                if g == 0:
                    for m in range(4):
                        if m < 3:
                            act.wait_ge(kv_mm, m + 1)
                        else:
                            act.wait_ge(blk_used, B_KV + 2)
                        nc.scalar.activation(kct[:, m, :], bank[m][:], ACT.Copy).then_inc(kv_copy, 1)
                elif g == 1:
                    flat_act(act, 0)
                if g:
                    for m in range(2):
                        act.wait_ge(kv_mm, 3 + 5 * (g - 1) + m + 1)
                        src = bank[((4, 5), (2, 3))[g - 1][m]]
                        for h in range(2):
                            part = slice(h * HD, (h + 1) * HD)
                            for o in range(2):
                                a = nc.scalar.activation(k2_hi[o * HD:(o + 1) * HD, g - 1, 2 * m + h, :],
                                                         src[part, :], ACT.Copy)
                            a.then_inc(kv_khi, 1)
                split_hi(act, B_KV + 2 * g + 1 + NSPLIT)

        def kv_dve(dve):
            nc.vector.memset(vsw[:, :, :, :, HD:VW], 1.0).then_inc(kv_v, 1)
            for i in range(TT):
                turn_dve(dve, turn_x, u_hi, u_lo, i)
            for g in range(3):
                split_lo(dve, B_KV + 2 * g + NSPLIT)
                if g:
                    for m in range(2):
                        src = bank[((4, 5), (2, 3))[g - 1][m]]
                        for h in range(2):
                            dve.wait_ge(kv_khi, 4 * (g - 1) + 2 * m + h + 1)
                            part = slice(h * HD, (h + 1) * HD)
                            for o in range(2):
                                a = nc.vector.tensor_tensor(k2_lo[o * HD:(o + 1) * HD, g - 1, 2 * m + h, :],
                                                            src[part, :],
                                                            k2_hi[part, g - 1, 2 * m + h, :].bitcast(F32),
                                                            ALU.subtract)
                            a.then_inc(kv_klo, 1)
                    for i in range(TT):
                        if i < TT - 1:
                            dve.wait_ge(kv_mm, 3 + 5 * (g - 1) + 2 + i + 1)
                        else:
                            dve.wait_ge(blk_used, B_KV + 2 * g + 2)
                        src = bank[((6, 7, 0, 1), (4, 5, 6, 7))[g - 1][i]]
                        nc.vector.tensor_copy(vsw[:, g - 1, i, :, 0:HD],
                                              src[:, 0:2 * P].rearrange("p (h d) -> p h d", d=HD)).then_inc(kv_v, 1)
                split_lo(dve, B_KV + 2 * g + 1 + NSPLIT)
                if g == 0:
                    flat_dve(dve, 0)
                if g == 1:
                    flat_lo_dve(dve, 0)

        def flat_dve(dve, i):
            dve.wait_ge(kv_copy, 2 * i + 2)
            if i:
                dve.wait_ge(fl_hi_made, 1)
                dve.wait_ge(blk_used, B_CMP + 2)
            n_made = 0
            for h in range(NKV):
                b0 = (h % 2) * HD
                kview = kct[b0:b0 + HD, 2 * i + h // 2, :].rearrange("p (n a b) -> p b a n", a=8, b=2)
                for half in range(2):
                    pe_col = (C_PE if h % 2 == half else C_PES) + 16 * i
                    for q in range(2):
                        pe = small[b0:b0 + HD, pe_col + 8 * q:pe_col + 8 * q + 8]
                        m = nc.vector.tensor_tensor(
                            fl[half * HD:(half + 1) * HD, 8 * q:8 * q + 8, h * NCMP:(h + 1) * NCMP],
                            kview[:, half, :, q:q + NCMP], pe.unsqueeze(2).to_broadcast([HD, 8, NCMP]), ALU.add)
            m.then_inc(fl_made, 1)

        def flat_act(act, i):
            act.wait_ge(fl_made, i + 1)
            if i:
                act.wait_ge(blk_used, B_CMP + 2)
            nc.scalar.activation(fl_hi[:], fl[:], ACT.Copy).then_inc(fl_hi_made, 1)

        def flat_lo_dve(dve, i):
            dve.wait_ge(fl_hi_made, i + 1)
            nc.vector.tensor_tensor(fl_lo[:], fl[:], fl_hi[:].bitcast(F32), ALU.subtract).then_inc(fl_lo_made, 1)

        def compress_pe(pe):
            for i in range(2):
                pe.wait_ge(fl_lo_made, i + 1)
                if i == 0:
                    pe.wait_ge(kv_v, 1 + 4)
                    pe.wait_ge(kv_klo, 8)
                for kh in range(2):
                    b = B_CMP + 2 * i + kh
                    pe.wait_ge(lo_done, b + 1)
                    wh = w_hi[:, b % NSPLIT, :].rearrange("p (k n) -> p k n", n=HC * P)
                    wl = w_lo[:, b % NRAW, :].rearrange("p (k n) -> p k n", n=HC * P)
                    for kk in range(8):
                        k = 8 * kh + kk
                        for hc in range(HC):
                            c_ = slice(hc * P, (hc + 1) * P)
                            mm = mm3(bank[2 * i + hc][:, 0:NC4], wh[:, kk, c_], wl[:, kk, c_], fl_hi[:, k, :],
                                     fl_lo[:, k, :], start=(k == 0), stop=(k == 15))
                    mm.then_inc(blk_used, 1)
            pe.wait_ge(att_in, 16 * 3)
            pe.wait_ge(kv_v, 1 + 8)
            for i in range(2):
                pe.wait_ge(gelu_made, 2 * (i + 1))
                if i == 0:
                    for hc in range(HC):
                        mm = nc.tensor.matmul(bank[4][0:HD, 0:NC4], w2[:, 0, hc, :], h1[:, 0, hc, :],
                                              start=(hc == 0), stop=(hc == HC - 1))
                else:
                    for h in range(NKV):
                        for hc in range(HC):
                            mm = nc.tensor.matmul(bank[5][0:NCMP, h * HD:(h + 1) * HD],
                                                  h1[:, 1, hc, h * NCMP:(h + 1) * NCMP], w2[:, 1, hc, :],
                                                  start=(hc == 0), stop=(hc == HC - 1))
                mm.then_inc(kc_mm, 1)

        def cmp_act(act):
            for i in range(2):
                split_hi(act, B_CMP + 2 * i + NSPLIT)
                act.wait_ge(blk_used, B_CMP + 2 * (i + 1))
                for hc in range(HC):
                    nc.scalar.activation(h1[:, i, hc, :], bank[2 * i + hc][:, 0:NC4], ACT.Gelu_apprx_tanh,
                                         bias=small[:, C_B1 + 2 * i + hc:C_B1 + 2 * i + hc + 1]).then_inc(gelu_made, 1)
                split_hi(act, B_CMP + 2 * i + 1 + NSPLIT)
                if i == 0:
                    flat_act(act, 1)
            act.wait_ge(kcf_made, 1)
            act.wait_ge(att_const, 8)
            for o in range(2):
                a = nc.scalar.activation(kc2_hi[o * HD:(o + 1) * HD, :, 0:NCMP],
                                         kcf[0:HD, :].rearrange("p (h n) -> p h n", n=NCMP), ACT.Copy)
            a.then_inc(kc_hi_made, 1)

        def cmp_dve(dve):
            split_lo(dve, B_CMP + NSPLIT)
            flat_dve(dve, 1)
            split_lo(dve, B_CMP + 1 + NSPLIT)
            flat_lo_dve(dve, 1)
            for b in range(B_CMP + 2, B_CMP + 4):
                split_lo(dve, b + NSPLIT)
            dve.wait_ge(kc_mm, 1)
            nc.vector.tensor_scalar(kcf[0:HD, :], bank[4][0:HD, 0:NC4], small[0:HD, C_B2:C_B2 + 1], None, ALU.add
                                    ).then_inc(kcf_made, 1)
            link(dve, dve_n, dve_step, nc.vector.memset(vc[:], 1.0))
            dve.wait_ge(kc_hi_made, 1)
            dve.wait_ge(att_const, 8)
            for o in range(2):
                nc.vector.tensor_tensor(kc2_lo[o * HD:(o + 1) * HD, :, 0:NCMP],
                                        kcf[0:HD, :].rearrange("p (h n) -> p h n", n=NCMP),
                                        kc2_hi[0:HD, :, 0:NCMP].bitcast(F32), ALU.subtract).then_inc(kc_made, 1)
            dve.wait_ge(kc_mm, 2)
            nc.vector.tensor_tensor(vc[0:NCMP, :, 0:HD], bank[5][0:NCMP, 0:NKV * HD].rearrange("p (h d) -> p h d", d=HD),
                                    bc(vb2[0:NCMP, :], [NCMP, NKV, HD], 1), ALU.add).then_inc(kc_made, 1)

        SCALE = HD ** -0.5
        def q_pe(pe):
            pe.wait_ge(kc_made, 3)
            for i in range(TT):
                turn_pe(pe, turn_q, us[:, i % 2, :], i)
            pe.wait_ge(*turn_q.lo.at(2 * TT))
            pe.wait_ge(wg_lo_made, 1)
            for k in range(KD):
                m = mm3(bank[6][0:3 * NH, :], wg_hi[:, k, :], wg_lo[:, k, :], u_hi[:, k, :], u_lo[:, k, :],
                        start=(k == 0), stop=(k == KD - 1))
            m.then_inc(gate_mm, 1)
            for g in range(2):
                for kh in range(2):
                    b = B_Q + 2 * g + kh
                    if g == 0 and kh == 1:
                        pe.wait_ge(gate_copied, 1)
                        for i in range(TT):
                            m = nc.tensor.transpose(bank[7][:, i * 3 * NH:(i + 1) * 3 * NH],
                                                    gate_t[0:3 * NH, i * P:(i + 1) * P], ident[0:3 * NH, 0:3 * NH])
                        m.then_inc(gate_turned, 1)
                    pe.wait_ge(lo_done, b + 1)
                    wh = w_hi[:, b % NSPLIT, :].rearrange("p (k n) -> p k n", k=4)
                    wl = w_lo[:, b % NRAW, :].rearrange("p (k n) -> p k n", k=4)
                    for m in range(4):
                        if kh == 0 and g == 1:
                            pe.wait_ge(q_lo, 2 * (m + 1))
                        for kk in range(4):
                            k = 4 * kh + kk
                            c_ = slice(m * P, (m + 1) * P)
                            mm = mm3(bank[m][:], wh[:, kk, c_], wl[:, kk, c_], u_hi[:, k, :], u_lo[:, k, :],
                                     start=(k == 0), stop=(k == KD - 1))
                        if kh == 1 and m < 3:
                            mm.then_inc(q_mm, 1)
                    mm.then_inc(blk_used, 1)

        def q_act(act):
            act.wait_ge(wg_in, 16)
            nc.scalar.activation(wg_hi[:], wg[:], ACT.Copy).then_inc(wg_hi_made, 1)
            for i in range(TT):
                turn_act(act, turn_q, u_hi, i)
            act.wait_ge(gate_mm, 1)
            nc.scalar.activation(gate_t[0:3 * NH, :], bank[6][0:3 * NH, :], ACT.Copy).then_inc(gate_copied, 1)
            act.wait_ge(gate_sum, 1)
            nc.scalar.activation(gates[:], gates[:], ACT.Sigmoid).then_inc(gate_sig, 1)
            for g in range(2):
                split_hi(act, B_Q + 2 * g + NSPLIT)
                for m in range(4):
                    if m < 3:
                        act.wait_ge(q_mm, 3 * g + m + 1)
                    else:
                        act.wait_ge(blk_used, B_Q + 2 * g + 2)
                    if g == 0 and m == 0:
                        act.wait_ge(gate_turned, 1)
                    for h in range(2):
                        part = slice(h * HD, (h + 1) * HD)
                        a = nc.scalar.activation(q2[part, 8 * g + 2 * m + h, :], bank[m][part, :], ACT.Copy,
                                                 scale=SCALE)
                        a.then_inc(q_hi, 1)
                split_hi(act, B_Q + 2 * g + 1 + NSPLIT)

        def q_dve(dve):
            for i in range(TT + 1):
                if i < TT:
                    modulate(dve, turn_q, 1, SC1, SH1, i)
                if i >= 1:
                    turn_dve(dve, turn_q, u_hi, u_lo, i - 1)
                if i == 1:
                    dve.wait_ge(wg_hi_made, 1)
                    nc.vector.tensor_tensor(wg_lo[:], wg[:], wg_hi[:].bitcast(F32), ALU.subtract).then_inc(wg_lo_made, 1)
            dve.wait_ge(gate_turned, 1)
            dve.wait_ge(att_in, 16 * 3)
            nc.vector.tensor_tensor(gates[:].rearrange("p i h j -> p i (h j)"),
                                    bank[7][:, 0:TT * 48].rearrange("p (i n) -> p i n", n=48),
                                    bc(bg[:], [P, TT, 48], 1), ALU.add).then_inc(gate_sum, 1)
            dve.wait_ge(x_saved, 16 * TT)
            dve.wait_ge(*turn_q.turned.at(2 * TT))
            ada_clear(dve, ada_b2, 0)
            dve.wait_ge(gate_sig, 1)
            dve.wait_ge(att_const, 8)
            nc.vector.tensor_scalar(gates[:, 0, :, 0:1], gates[:, 0, :, 0:1], has_c[:, 0:1], None, ALU.mult
                                    ).then_inc(gate_made, 1)
            for g in range(2):
                split_lo(dve, B_Q + 2 * g + NSPLIT)
                for m in range(4):
                    for h in range(2):
                        dve.wait_ge(q_hi, 8 * g + 2 * m + h + 1)
                        part, other = slice(h * HD, (h + 1) * HD), slice((1 - h) * HD, (2 - h) * HD)
                        head = 8 * g + 2 * m + h
                        nc.vector.scalar_tensor_tensor(out=q2[other, head, :], in0=bank[m][part, :], scalar=SCALE,
                                                       in1=q2[part, head, :].bitcast(F32), op0=ALU.mult,
                                                       op1=ALU.subtract).then_inc(q_lo, 1)
                split_lo(dve, B_Q + 2 * g + 1 + NSPLIT)

        UNITS = NH * TT
        TILE = (3, 0, 2, 1)
        (att_s, att_nm, att_exp, att_t, att_ts, att_tw, att_o, att_done) = (
            sem("att_" + n) for n in ("s", "nm", "exp", "t", "ts", "tw", "o", "done"))
        attc_s, attc_sub, attc_exp, attc_t, attc_ts = (sem("attc_" + n) for n in ("s", "sub", "exp", "t", "ts"))

        def scores_pe(pe, u):
            h, i = u // TT, TILE[u % TT]
            if u >= 2:
                pe.wait_ge(att_exp, 2 * (u - 1))
            n = (i + 1) * P
            q = q2[:, h, i * P:(i + 1) * P]
            for br in (SEL, WIN):
                o = bank[2 * (u % 2) + br]
                nc.tensor.matmul(o[:, 0:n], q, k2_hi[:, br, h // GQA, 0:n], start=True, stop=False)
                nc.tensor.matmul(o[:, 0:n], q, k2_lo[:, br, h // GQA, 0:n], start=False, stop=False)
                m = nc.tensor.matmul(o[:, i * P:n], identb[:], causal[:], start=False, stop=True)
            m.then_inc(att_s, 1)

        def cscores_pe(pe, h):
            if h >= 1:
                pe.wait_ge(attc_ts, h)
            for i in range(TT):
                o = bank[4][:, i * 32:(i + 1) * 32]
                q = q2[:, h, i * P:(i + 1) * P]
                nc.tensor.matmul(o, q, kc2_hi[:, h // GQA, :], start=True, stop=False)
                nc.tensor.matmul(o, q, kc2_lo[:, h // GQA, :], start=False, stop=False)
                m = nc.tensor.matmul(o, identb[:], causal_c[:, i, :], start=False, stop=True)
            m.then_inc(attc_s, 1)

        def cturn_pe(pe, h):
            pe.wait_ge(attc_exp, h + 1)
            for i in range(TT):
                m = nc.tensor.transpose(bank[4][0:NCMP, i * P:(i + 1) * P], prob_c[:, h % 2, i, 0:NCMP], ident[:])
            m.then_inc(attc_t, 1)

        def turn_probs_pe(pe, u):
            h, i = u // TT, TILE[u % TT]
            pe.wait_ge(att_exp, 2 * (u + 1))
            for br in (SEL, WIN):
                if u >= 1:
                    pe.wait_ge((att_ts, att_tw)[br], u)
                for k in range(i + 1):
                    m = nc.tensor.transpose(bank[5 + br][:, k * P:(k + 1) * P], prob[:, u % 2, br, k * P:(k + 1) * P],
                                            ident[:])
                m.then_inc(att_t, 1)

        def values_pe(pe, u):
            h, i = u // TT, TILE[u % TT]
            pe.wait_ge(att_tw, u + 1)
            pe.wait_ge(att_ts, u + 1)
            pe.wait_ge(attc_ts, h + 1)
            if u >= 1:
                pe.wait_ge(att_done, u)
            nc.tensor.matmul(bank[7][:, 0:VW], prob_ct[0:NCMP, h % 2, i * P:(i + 1) * P], vc[0:NCMP, h // GQA, :],
                             start=True, stop=True)
            for br in (SEL, WIN):
                for k in range(i + 1):
                    m = nc.tensor.matmul(bank[7][:, (1 + br) * VW:(2 + br) * VW],
                                         prob_t[:, u % 2, br, k * P:(k + 1) * P], vsw[:, br, k, h // GQA, :],
                                         start=(k == 0), stop=(k == i))
            m.then_inc(att_o, 1)

        def attention_pe(pe):
            pe.wait_ge(q_lo, 16)
            pe.wait_ge(att_const, 8)
            pe.wait_ge(gate_made, 1)
            pe.wait_ge(kv_v, 1 + 8)
            cscores_pe(pe, 0)
            for t in range(UNITS + 2):
                if t < UNITS:
                    scores_pe(pe, t)
                    if t == 1:
                        cturn_pe(pe, 0)
                    if t % TT == 1 and t // TT + 1 < NH:
                        cscores_pe(pe, t // TT + 1)
                    if t % TT == 3 and t // TT + 1 < NH:
                        cturn_pe(pe, t // TT + 1)
                if 1 <= t <= UNITS:
                    turn_probs_pe(pe, t - 1)
                if t >= 2:
                    values_pe(pe, t - 2)

        def cexp_act(act, h):
            act.wait_ge(attc_sub, h + 1)
            nc.scalar.activation(prob_c[:, h % 2, :, :], prob_c[:, h % 2, :, :], ACT.Exp).then_inc(attc_exp, 1)

        def cturn_act(act, h):
            act.wait_ge(attc_t, h + 1)
            if h >= 2:
                act.wait_ge(att_o, TT * (h - 1))
            nc.scalar.activation(prob_ct[0:NCMP, h % 2, :], bank[4][0:NCMP, :], ACT.Copy).then_inc(attc_ts, 1)

        def attention_act(act):
            cexp_act(act, 0)
            for t in range(UNITS + 1):
                if t < UNITS:
                    n = (TILE[t % TT] + 1) * P
                    act.wait_ge(att_nm, t + 1)
                    if t >= 2:
                        act.wait_ge(att_t, 2 * (t - 1))
                    for br in (SEL, WIN):
                        nc.scalar.activation(prob[:, t % 2, br, 0:n], bank[2 * (t % 2) + br][:, 0:n], ACT.Exp,
                                             bias=snm[:, t % 2, br:br + 1]).then_inc(att_exp, 1)
                    if t == 1:
                        cturn_act(act, 0)
                    if t % TT == 1 and t // TT + 1 < NH:
                        cexp_act(act, t // TT + 1)
                    if t % TT == 3 and t // TT + 1 < NH:
                        cturn_act(act, t // TT + 1)
                if t >= 1:
                    u = t - 1
                    n = (TILE[u % TT] + 1) * P
                    act.wait_ge(att_t, 2 * u + 1)
                    if u >= 2:
                        act.wait_ge(att_o, u - 1)
                    nc.scalar.activation(prob_t[:, u % 2, SEL, 0:n], bank[5][:, 0:n], ACT.Copy).then_inc(att_ts, 1)

        def cmax_dve(dve, h):
            dve.wait_ge(attc_s, h + 1)
            if h >= 2:
                dve.wait_ge(attc_t, h - 1)
            s_ = bank[4][:, 0:TT * 32].rearrange("p (i n) -> p i n", n=32)
            link(dve, dve_n, dve_step, nc.vector.tensor_reduce(cmax[:], s_, AX_X, ALU.max))
            nc.vector.tensor_tensor(prob_c[:, h % 2, :, :], s_, bc(cmax[:], [P, TT, 32], 2), ALU.subtract
                                    ).then_inc(attc_sub, 1)

        def attention_dve(dve):
            cmax_dve(dve, 0)
            for t in range(UNITS + 2):
                if t < UNITS:
                    n = (TILE[t % TT] + 1) * P
                    dve.wait_ge(att_s, t + 1)
                    if t >= 2:
                        dve.wait_ge(att_exp, 2 * (t - 1))
                    for br in (SEL, WIN):
                        m = nc.vector.tensor_reduce(snm[:, t % 2, br:br + 1], bank[2 * (t % 2) + br][:, 0:n], AX_X,
                                                    ALU.max, negate=True)
                    m.then_inc(att_nm, 1)
                    if t % TT == 1 and t // TT + 1 < NH:
                        cmax_dve(dve, t // TT + 1)
                if 1 <= t <= UNITS:
                    u = t - 1
                    n = (TILE[u % TT] + 1) * P
                    dve.wait_ge(att_t, 2 * u + 2)
                    if u >= 2:
                        dve.wait_ge(att_o, u - 1)
                    nc.vector.tensor_copy(prob_t[:, u % 2, WIN, 0:n], bank[6][:, 0:n]).then_inc(att_tw, 1)
                if t >= 2:
                    u = t - 2
                    h, i = u // TT, TILE[u % TT]
                    dve.wait_ge(att_o, u + 1)
                    o3 = bank[7][:, 0:3 * VW].rearrange("p (b v) -> p b v", v=VW)
                    rec = orec[:, u % 2, :]
                    link(dve, dve_n, dve_step, nc.vector.reciprocal(rec, o3[:, :, HD]))
                    link(dve, dve_n, dve_step, nc.vector.tensor_tensor(rec, rec, gates[:, i, h, :], ALU.mult))
                    dst = o_tok[:, i, h * HD:(h + 1) * HD]
                    tmp3 = otmp[:, u % 2, :, :]
                    link(dve, dve_n, dve_step, nc.vector.tensor_tensor(tmp3, o3[:, :, 0:HD], bc(rec, [P, 3, HD], 2),
                                                                       ALU.mult))
                    nc.vector.tensor_reduce(dst, tmp3.rearrange("p b v -> p v b"), AX_X, ALU.add).then_inc(att_done, 1)
                if t % 2 == 1:
                    ada_macs(dve, ada_b2, t // 2, 1)

        wo = Proj("wo", B_O)

        def att_pe(pe):
            kv_pe(pe)
            compress_pe(pe)
            q_pe(pe)
            attention_pe(pe)
            for i in range(TT):
                if i == 0:
                    pe.wait_ge(att_done, UNITS)
                turn_pe(pe, turn_o, o_tok[:, i, :], i)

            def free(n):
                if n == 0:
                    pe.wait_ge(*turn_o.lo.at(2 * TT))
                    for j in range(8, 12):
                        mod_sums(pe, ada_b2, j, bank[4:6])
                else:
                    pe.wait_ge(*ada_b2.row_made.at(8))
            proj_pe(pe, wo, B_O, free)

        def att_act(act):
            kv_act(act)
            cmp_act(act)
            q_act(act)
            attention_act(act)
            for i in range(TT):
                turn_act(act, turn_o, v_hi, i)
            for j in range(8, 12):
                mod_rows(act, ada_b2, j, bank[4:6])
                mod_store(act, ada_b2, j)
            proj_norm_act(act, norms[1, 0], B_O)

        def att_dve(dve):
            kv_dve(dve)
            cmp_dve(dve)
            q_dve(dve)
            attention_dve(dve)
            dve.wait_ge(att_done, UNITS)
            dve.sem_inc(turn_o.ready.sem, TT)
            for i in range(TT):
                turn_dve(dve, turn_o, v_hi, v_lo, i)
            proj_norm_dve(dve, wo, norms[1, 0], B_O, 2)

        def att_pool(pool):
            pool.wait_ge(*norms[0, 1].done.at(TT))
            nc.gpsimd.memset(causal[:], 0.0).then_inc(att_const, 1)
            nc.gpsimd.memset(causal_c[:], 0.0).then_inc(att_const, 1)
            nc.gpsimd.memset(has_c[:], 1.0).then_inc(att_const, 1)
            nc.gpsimd.memset(kc2_hi[:].bitcast(F32), 0.0).then_inc(att_const, 1)
            nc.gpsimd.memset(kc2_lo[:].bitcast(F32), 0.0).then_inc(att_const, 1)
            pool.wait_ge(att_const, 5)
            nc.gpsimd.affine_select(out=causal[:], in_=causal[:], compare_op=ALU.is_ge, fill=NEG, base=0,
                                    pattern=[[-1, P]], channel_multiplier=1).then_inc(att_const, 1)
            nc.gpsimd.affine_select(out=causal_c[:], in_=causal_c[:], compare_op=ALU.is_ge, fill=NEG,
                                    base=-(CMP_BLOCK - 1), pattern=[[P, TT], [-CMP_STRIDE, 32]],
                                    channel_multiplier=1).then_inc(att_const, 1)
            nc.gpsimd.affine_select(out=has_c[:], in_=has_c[:], compare_op=ALU.is_ge, fill=0.0,
                                    base=-(CMP_BLOCK - 1), pattern=[[0, 1]], channel_multiplier=1).then_inc(att_const, 1)
            pool.wait_ge(blk_used, B_CMP)
            pool.dma_start(w2[:], cmp_w2.rearrange("i (c p) d -> p i c d", p=P)).then_inc(att_in, 16)
            pool.dma_start(vb2[:], cmp_b2[1].partition_broadcast(P)).then_inc(att_in, 16)
            pool.dma_start(bg[:], b_g[0].partition_broadcast(P)).then_inc(att_in, 16)
            pool.wait_ge(blk_used, B_Q)
            pool.dma_start(wg[:], w_qg[0].rearrange("(k p) n -> p k n", p=P)[:, :, D:D + 3 * NH]).then_inc(wg_in, 16)
            pool.wait_ge(blk_used, B_O)
            for j in range(8, 12):
                ada_loads(pool, ada_b2, j)
            pool.wait_ge(att_done, UNITS)
            row_load(pool, R[("mod", 1, G1)])
            row_load(pool, R[("g", 1, 0)])
            row_load(pool, R[("b", 1, 0)])
            norm_shifts(pool, norms[1, 0], [("mod", 1, SC2), ("mod", 1, SH2)])

        def att_sp(sp):
            for b in range(3, 6):
                load_block(sp, B_KV + b, kv[b])
            for i in range(TT):
                sp.wait_ge(*norms[0, 1].done.at(i + 1))
                sp.dma_start(scratch["x"][i * P:(i + 1) * P, :], xt[:, i, :]).then_inc(x_saved, 16)
            for b in range(4):
                load_block(sp, B_CMP + b, cmp1[b])
            for b in range(4):
                load_block(sp, B_Q + b, qw[b])
            for b in range(4):
                load_block(sp, B_O + b, ow[b])
            sp.wait_ge(*ada_b2.stored.at(16 * 4))
            for i in range(TT):
                sp.dma_start(xt[:, i, :], scratch["x"][i * P:(i + 1) * P, :]).then_inc(x_back, 16)

        block = ctx.enter_context(nc.Block())

        @block.sync
        def _(sp):
            for i in range(TT):
                sp.dma_start(xt[:, i, :], x[0, i * P:(i + 1) * P, :]).then_inc(x_in, 16)
            sp.wait_ge(*ada_a.mac.at(12))
            for b, src in enumerate(conv_in):
                load_block(sp, b, src)
            for b in range(4):
                load_block(sp, B_COUT + b, conv_out[b])
            sp.wait_ge(conv_lo, 8)
            for i in range(TT):
                sp.dma_start(xt[:, i, :], x[0, i * P:(i + 1) * P, :]).then_inc(x_back, 16)
            moe_sp(sp, moes[0], [(B_KV + b, kv[b]) for b in range(3)])
            att_sp(sp)
            moe_sp(sp, moes[1], [])
            for i in range(TT):
                sp.wait_ge(*norms[1, 1].done.at(i + 1))
                sp.dma_start(out[0, i * P:(i + 1) * P, :], xt[:, i, :]).then_inc(stored, 16)
            sp.wait_ge(stored, 16 * TT)

        @block.gpsimd
        def _(pool):
            constants(pool)
            ada_loads(pool, ada_a, 0)
            ada_loads(pool, ada_a, 1)
            row_load(pool, 0)
            row_load(pool, 1)
            for j in range(2, 8):
                ada_loads(pool, ada_a, j)
            for r in range(2, 5):
                row_load(pool, r)
            norm_shifts(pool, norms[0, 0], [("mod", 0, SC2), ("mod", 0, SH2)])
            moe_pool(pool, moes[0])
            att_pool(pool)
            moe_pool(pool, moes[1])

        @block.scalar
        def _(act):
            small_loads(act)
            act.wait_ge(small_ready, 1)
            nc.scalar.activation(silu_c[:], small[:, C_C:C_C + KD], ACT.Silu).then_inc(silu_ready, 1)
            mod_rows(act, ada_a, 0, bank[4:6])
            mod_store(act, ada_a, 0)
            mod_rows(act, ada_a, 1, bank[4:6])
            mod_store(act, ada_a, 1)
            for b in range(NSPLIT):
                split_hi(act, b)
            for i in range(TT):
                turn_act(act, turn_u, u_hi, i)
            conv_act(act)
            proj_norm_act(act, norms[0, 0], B_COUT)
            moe_act(act, moes[0])
            att_act(act)
            moe_act(act, moes[1])

        @block.vector
        def _(dve):
            nc.vector.memset(small_rows[:], 0.0).then_inc(small_clear, 1)
            nc.vector.memset(bias0[:], 0.0).then_inc(ada_a.cleared.sem, 1)
            nc.vector.memset(ones_col[:], 1.0).then_inc(const_v, 1)
            nc.vector.memset(eps_col[:], LN_EPS).then_inc(const_v, 1)
            dve.wait_ge(small_t, 1)
            nc.vector.tensor_copy(small[:], bank[0][:, 0:P]).then_inc(small_ready, 1)
            dve.wait_ge(silu_ready, 1)
            ada_macs(dve, ada_a, 0, MACS_FIRST)
            for b in range(NSPLIT):
                split_lo(dve, b)
            dve.wait_ge(x_in, 16 * TT)
            for i in range(TT + 1):
                if i < TT:
                    modulate(dve, turn_u, 0, SC1, SH1, i)
                if i >= 1:
                    turn_dve(dve, turn_u, u_hi, u_lo, i - 1)
            dve.wait_ge(*turn_u.turned.at(2 * TT))
            nc.vector.memset(z[:, :, 0:2], 0.0).then_inc(const_v, 1)
            dve.wait_ge(const_v, 3)
            conv_dve(dve)
            proj_norm_dve(dve, cout, norms[0, 0], B_COUT, 1)
            moe_dve(dve, moes[0])
            att_dve(dve)
            moe_dve(dve, moes[1])

        @block.tensor
        def _(pe):
            pe.wait_ge(const_step, N_CONST)
            pe.wait_ge(small_in, 16 * N_SMALL)
            nc.tensor.transpose(bank[0][:, 0:P], small_rows[:], ident[:]).then_inc(small_t, 1)
            pe.wait_ge(const_v, 2)
            mod_sums(pe, ada_a, 0, bank[4:6])
            mod_sums(pe, ada_a, 1, bank[4:6])
            pe.wait_ge(*ada_a.row_made.at(4))
            for i in range(TT):
                turn_pe(pe, turn_u, us[:, i % 2, :], i)
            pe.wait_ge(small_ready, 1)
            pe.wait_ge(*turn_u.lo.at(2 * TT))
            conv_pe(pe)
            moe_pe(pe, moes[0])
            att_pe(pe)
            moe_pe(pe, moes[1])


_INS = ['x', 'c', 'ada_w', 'ada_b', 'ln_g', 'ln_b', 'conv_w_in', 'conv_w', 'conv_b', 'conv_w_out', 'w_kv', 'cmp_pe',
        'cmp_w1', 'cmp_b1', 'cmp_w2', 'cmp_b2', 'w_qg', 'b_g', 'w_o', 'router_w', 'router_bias', 'w_gu', 'w_down']


def kernel(**inputs):
    import numpy as _np
    import concourse.bacc as _bacc
    from concourse.bass_utils import run_bass_kernel_spmd as _run

    nc = _bacc.Bacc("TRN2", target_bir_lowering=False, num_devices=1)
    arrays, args = {}, []
    for name in _INS:
        a = _np.ascontiguousarray(inputs[name])
        arrays[f"in_{name}_dram"] = a
        args.append(nc.dram_tensor(f"in_{name}_dram", a.shape, F32, kind="ExternalInput").ap())
    out = nc.dram_tensor("out_0_dram", (1, SEQ, D), F32, kind="ExternalOutput").ap()
    scratch = {name: nc.dram_tensor(f"scratch_{name}", shape, F32, kind="Internal").ap() for name, shape in
               (("mods", (6 * DEPTH, D)), ("u0", (SEQ, D)), ("u1", (SEQ, D)),
                ("y0", (NE * CAP, D)), ("y1", (NE * CAP, D)), ("x", (SEQ, D)))}
    hybrid_trunk(nc, *args, out, scratch)
    r = _run(nc, [arrays], core_ids=[0])
    return r.results[0]["out_0_dram"]
```
